# Optimizing a Trainium2 kernel written in Bass

```python
import math
import jax, jax.numpy as jnp
from jax import lax
import numpy as np

D_MODEL = 1024
BATCH = 1
SEQ = 1024
DEPTH = 1

MIX_WIDTH = D_MODEL
D_RG = MIX_WIDTH // 2
D_S5 = MIX_WIDTH - D_RG
RG_HEADS = 8
RG_HD = D_RG // RG_HEADS
CONV_W = 4
RG_C = 8.0
S5_CH = 16
S5_GROUPS = D_S5 // S5_CH
S5_STATE = 64
MEM_LEN = 256
XA_HEADS = 4
XA_HD = D_MODEL // XA_HEADS
N_EXPERTS = 32
TOP_K = 4
D_FF = D_MODEL
SWIGLU_LIMIT = 7.0
SWIGLU_ALPHA = 1.702
MOE_BLOCK = 128
NORM_EPS = 1e-6

kernel_name = "hymba_rglru_s5_memxattn_moe"

def rmsnorm(x, g):
    xf = x.astype(jnp.float32)
    y = xf * lax.rsqrt(jnp.mean(xf * xf, axis=-1, keepdims=True) + NORM_EPS)
    return (y * g.astype(jnp.float32)).astype(x.dtype)

def causal_depthwise_conv(x, w, b):
    s = x.shape[1]
    xp = jnp.pad(x, ((0, 0), (CONV_W - 1, 0), (0, 0)))
    y = xp[:, 0:s] * w[0]
    for k in range(1, CONV_W):
        y = y + xp[:, k:k + s] * w[k]
    return y + b

def _linear_combine(c1, c2):
    a1, b1 = c1
    a2, b2 = c2
    return a1 * a2, a2 * b1 + b2

def rg_lru_mixer(xa, gate, conv_w, conv_b, rg_wa, rg_ba, rg_wx, rg_bx, rg_lambda):
    bsz, s, _ = xa.shape
    xc = causal_depthwise_conv(xa, conv_w, conv_b)
    xh = xc.reshape(bsz, s, RG_HEADS, RG_HD)
    r = jax.nn.sigmoid(jnp.einsum('bshi,hij->bshj', xh, rg_wa).reshape(bsz, s, D_RG) + rg_ba)
    i = jax.nn.sigmoid(jnp.einsum('bshi,hij->bshj', xh, rg_wx).reshape(bsz, s, D_RG) + rg_bx)
    log_a = -RG_C * r * jax.nn.softplus(-rg_lambda)
    a = jnp.exp(log_a)
    mult = jnp.sqrt(-jnp.expm1(2.0 * log_a))
    is_start = (jnp.arange(s) == 0)[None, :, None]
    mult = jnp.where(is_start, jnp.ones_like(mult), mult)
    b = mult * (i * xc)
    _, h = lax.associative_scan(_linear_combine, (a, b), axis=1)
    return h * jax.nn.gelu(gate)

def _complex_linear_combine(c1, c2):
    ar1, ai1, br1, bi1 = c1
    ar2, ai2, br2, bi2 = c2
    ar = ar2 * ar1 - ai2 * ai1
    ai = ar2 * ai1 + ai2 * ar1
    br = ar2 * br1 - ai2 * bi1 + br2
    bi = ar2 * bi1 + ai2 * br1 + bi2
    return ar, ai, br, bi

def s5_mixer(u, lam_re, lam_im, b_re, b_im, c_re, c_im, d_skip, log_dt, glu_w, glu_b):
    bsz, s, _ = u.shape
    ug = u.reshape(bsz, s, S5_GROUPS, S5_CH)
    dt = jnp.exp(log_dt)[:, None]
    mag = jnp.exp(dt * lam_re)
    abar_re = mag * jnp.cos(dt * lam_im)
    abar_im = mag * jnp.sin(dt * lam_im)
    den = lam_re * lam_re + lam_im * lam_im
    num_re = abar_re - 1.0
    coef_re = (num_re * lam_re + abar_im * lam_im) / den
    coef_im = (abar_im * lam_re - num_re * lam_im) / den
    bbar_re = coef_re[..., None] * b_re - coef_im[..., None] * b_im
    bbar_im = coef_re[..., None] * b_im + coef_im[..., None] * b_re
    bu_re = jnp.einsum('bsgc,gpc->bsgp', ug, bbar_re)
    bu_im = jnp.einsum('bsgc,gpc->bsgp', ug, bbar_im)
    ar = jnp.broadcast_to(abar_re[None, None], (1, s, S5_GROUPS, S5_STATE)).astype(bu_re.dtype)
    ai = jnp.broadcast_to(abar_im[None, None], (1, s, S5_GROUPS, S5_STATE)).astype(bu_re.dtype)
    _, _, h_re, h_im = lax.associative_scan(_complex_linear_combine, (ar, ai, bu_re, bu_im), axis=1)
    y = (jnp.einsum('bsgp,gcp->bsgc', h_re, c_re) - jnp.einsum('bsgp,gcp->bsgc', h_im, c_im)
         + d_skip.reshape(S5_GROUPS, S5_CH) * ug)
    z = jax.nn.gelu(y)
    gate = jax.nn.sigmoid(jnp.einsum('bsgc,gcd->bsgd', z, glu_w) + glu_b.reshape(S5_GROUPS, S5_CH))
    return (z * gate).reshape(bsz, s, D_S5)

def memory_cross_attention(xn, mem, mem_g, xa_wq, xa_wkv, xa_wo):
    bsz, s, _ = xn.shape
    m = mem.shape[1]
    q = (xn @ xa_wq).reshape(bsz, s, XA_HEADS, XA_HD)
    kv = (rmsnorm(mem, mem_g) @ xa_wkv).reshape(bsz, m, 2, XA_HEADS, XA_HD)
    k, v = kv[:, :, 0], kv[:, :, 1]
    scores = jnp.einsum('bshd,bmhd->bhsm', q, k).astype(jnp.float32) * (XA_HD ** -0.5)
    p = jax.nn.softmax(scores, axis=-1).astype(v.dtype)
    o = jnp.einsum('bhsm,bmhd->bshd', p, v).reshape(bsz, s, D_MODEL)
    return o @ xa_wo

def clamped_swiglu_expert(xb, w_gu, b_gu, w_down, b_down):
    gu = xb @ w_gu + b_gu
    g, u = gu[:, :D_FF], gu[:, D_FF:]
    g = jnp.minimum(g, SWIGLU_LIMIT)
    u = jnp.clip(u, -SWIGLU_LIMIT, SWIGLU_LIMIT)
    h = (u + 1.0) * (g * jax.nn.sigmoid(SWIGLU_ALPHA * g))
    return h @ w_down + b_down

def moe_ffn(xn, router_w, router_b, exp_w_gu, exp_b_gu, exp_w_down, exp_b_down):
    bsz, s, d = xn.shape
    n = bsz * s
    xt = xn.reshape(n, d)
    logits = (xt @ router_w + router_b).astype(jnp.float32)
    top_val, top_idx = lax.top_k(logits, TOP_K)
    gates = jax.nn.softmax(top_val, axis=-1).astype(xt.dtype)
    n_assign = n * TOP_K
    e_flat = top_idx.reshape(n_assign)
    t_flat = jnp.repeat(jnp.arange(n, dtype=jnp.int32), TOP_K)
    w_flat = gates.reshape(n_assign)
    order = jnp.argsort(e_flat)
    e_s, t_s, w_s = e_flat[order], t_flat[order], w_flat[order]
    counts = jnp.bincount(e_flat, length=N_EXPERTS)
    padded = ((counts + MOE_BLOCK - 1) // MOE_BLOCK) * MOE_BLOCK
    start = jnp.cumsum(counts) - counts
    pend = jnp.cumsum(padded)
    pstart = pend - padded
    dest = pstart[e_s] + (jnp.arange(n_assign) - start[e_s])
    n_slots = n_assign + N_EXPERTS * MOE_BLOCK
    n_blocks = n_slots // MOE_BLOCK
    slot_tok = jnp.zeros((n_slots,), jnp.int32).at[dest].set(t_s)
    slot_w = jnp.zeros((n_slots,), xt.dtype).at[dest].set(w_s)
    block_exp = jnp.minimum(
        jnp.searchsorted(pend, jnp.arange(n_blocks) * MOE_BLOCK, side='right'), N_EXPERTS - 1)

    def run_block(args):
        tok, e = args
        return clamped_swiglu_expert(xt[tok], exp_w_gu[e], exp_b_gu[e], exp_w_down[e], exp_b_down[e])

    yb = lax.map(run_block, (slot_tok.reshape(n_blocks, MOE_BLOCK), block_exp))
    y = jnp.zeros((n, d), xt.dtype).at[slot_tok].add(yb.reshape(n_slots, d) * slot_w[:, None])
    return y.reshape(bsz, s, d)

def setup_inputs(seed: int = 0) -> dict:
    key = jax.random.key(seed)
    ks = jax.random.split(key, 40)
    f32 = jnp.float32
    nrm = lambda k, shape, scale: jax.random.normal(k, shape, f32) * scale
    gain = lambda k, n: 1.0 + 0.01 * jax.random.normal(k, (n,), f32)
    a0 = jax.random.uniform(ks[10], (D_RG,), f32, 0.9, 0.999)
    sa = a0 ** (1.0 / RG_C)
    rg_lambda = jnp.log(sa) - jnp.log1p(-sa)
    n_idx = jnp.arange(S5_STATE, dtype=f32)
    lam_re = -0.5 + 0.01 * jax.random.normal(ks[11], (S5_GROUPS, S5_STATE), f32)
    lam_im = jnp.pi * n_idx[None, :] + 0.01 * jax.random.normal(ks[12], (S5_GROUPS, S5_STATE), f32)
    log_dt = jax.random.uniform(ks[13], (S5_GROUPS,), f32, math.log(0.001), math.log(0.1))
    return {
        "x": jax.random.normal(ks[0], (BATCH, SEQ, D_MODEL), f32),
        "mem": jax.random.normal(ks[1], (BATCH, MEM_LEN, D_MODEL), f32),
        "norm_mix_g": gain(ks[2], D_MODEL),
        "w_in": nrm(ks[3], (D_MODEL, 2 * D_RG + D_S5), D_MODEL ** -0.5),
        "conv_w": nrm(ks[4], (CONV_W, D_RG), CONV_W ** -0.5),
        "conv_b": nrm(ks[5], (D_RG,), 0.01),
        "rg_wa": nrm(ks[6], (RG_HEADS, RG_HD, RG_HD), RG_HD ** -0.5),
        "rg_ba": nrm(ks[7], (D_RG,), 0.01),
        "rg_wx": nrm(ks[8], (RG_HEADS, RG_HD, RG_HD), RG_HD ** -0.5),
        "rg_bx": nrm(ks[9], (D_RG,), 0.01),
        "rg_lambda": rg_lambda,
        "s5_lambda_re": lam_re,
        "s5_lambda_im": lam_im,
        "s5_b_re": nrm(ks[14], (S5_GROUPS, S5_STATE, S5_CH), (2.0 * S5_CH) ** -0.5),
        "s5_b_im": nrm(ks[15], (S5_GROUPS, S5_STATE, S5_CH), (2.0 * S5_CH) ** -0.5),
        "s5_c_re": nrm(ks[16], (S5_GROUPS, S5_CH, S5_STATE), (S5_STATE) ** -0.5),
        "s5_c_im": nrm(ks[17], (S5_GROUPS, S5_CH, S5_STATE), (S5_STATE) ** -0.5),
        "s5_d": nrm(ks[18], (D_S5,), 1.0),
        "s5_log_dt": log_dt,
        "s5_glu_w": nrm(ks[19], (S5_GROUPS, S5_CH, S5_CH), S5_CH ** -0.5),
        "s5_glu_b": nrm(ks[20], (D_S5,), 0.01),
        "w_out": nrm(ks[21], (MIX_WIDTH, D_MODEL), MIX_WIDTH ** -0.5),
        "norm_xa_g": gain(ks[22], D_MODEL),
        "mem_norm_g": gain(ks[23], D_MODEL),
        "xa_wq": nrm(ks[24], (D_MODEL, D_MODEL), D_MODEL ** -0.5),
        "xa_wkv": nrm(ks[25], (D_MODEL, 2 * D_MODEL), D_MODEL ** -0.5),
        "xa_wo": nrm(ks[26], (D_MODEL, D_MODEL), D_MODEL ** -0.5),
        "norm_ffn_g": gain(ks[27], D_MODEL),
        "router_w": nrm(ks[28], (D_MODEL, N_EXPERTS), D_MODEL ** -0.5),
        "router_b": nrm(ks[29], (N_EXPERTS,), 0.01),
        "exp_w_gu": nrm(ks[30], (N_EXPERTS, D_MODEL, 2 * D_FF), D_MODEL ** -0.5),
        "exp_b_gu": nrm(ks[31], (N_EXPERTS, 2 * D_FF), 0.01),
        "exp_w_down": nrm(ks[32], (N_EXPERTS, D_FF, D_MODEL), D_FF ** -0.5),
        "exp_b_down": nrm(ks[33], (N_EXPERTS, D_MODEL), 0.01),
        "final_norm_g": gain(ks[34], D_MODEL),
    }

def reference(x, mem, norm_mix_g, w_in, conv_w, conv_b, rg_wa, rg_ba, rg_wx, rg_bx, rg_lambda,
              s5_lambda_re, s5_lambda_im, s5_b_re, s5_b_im, s5_c_re, s5_c_im, s5_d, s5_log_dt,
              s5_glu_w, s5_glu_b, w_out, norm_xa_g, mem_norm_g, xa_wq, xa_wkv, xa_wo,
              norm_ffn_g, router_w, router_b, exp_w_gu, exp_b_gu, exp_w_down, exp_b_down,
              final_norm_g):
    h = x
    for _ in range(DEPTH):
        xn = rmsnorm(h, norm_mix_g)
        proj = xn @ w_in
        gate_rg = proj[..., :D_RG]
        x_rg = proj[..., D_RG:2 * D_RG]
        u_s5 = proj[..., 2 * D_RG:]
        y_rg = rg_lru_mixer(x_rg, gate_rg, conv_w, conv_b, rg_wa, rg_ba, rg_wx, rg_bx, rg_lambda)
        y_s5 = s5_mixer(u_s5, s5_lambda_re, s5_lambda_im, s5_b_re, s5_b_im, s5_c_re, s5_c_im,
                        s5_d, s5_log_dt, s5_glu_w, s5_glu_b)
        h = h + jnp.concatenate([y_rg, y_s5], axis=-1) @ w_out
        h = h + memory_cross_attention(rmsnorm(h, norm_xa_g), mem, mem_norm_g, xa_wq, xa_wkv, xa_wo)
        h = h + moe_ffn(rmsnorm(h, norm_ffn_g), router_w, router_b, exp_w_gu, exp_b_gu,
                        exp_w_down, exp_b_down)
    return rmsnorm(h, final_norm_g)


_drawn_inputs = setup_inputs


def setup_inputs(seed=0):
    import zlib

    import numpy as np

    out = dict(_drawn_inputs(seed))
    spreads = {}
    factors = {'norm_mix_g': 2.696,
     'rg_ba': 8.0,
     'rg_bx': 6.383,
     's5_lambda_re': 64.0,
     's5_glu_b': 8.0,
     'norm_xa_g': 6.858,
     'mem_norm_g': 5.969,
     'exp_b_gu': 61.479,
     'exp_b_down': 64.0,
     'final_norm_g': 32.336,
     'norm_ffn_g': 8.0,
     'router_b': 8.0}
    for name, (base, spread) in spreads.items():
        noise = np.random.default_rng([zlib.crc32(name.encode()), seed]).standard_normal(out[name].shape)
        drawn = base * np.exp(spread * noise) if base else spread * noise
        out[name] = __import__('jax').numpy.asarray(drawn.astype(out[name].dtype))
    for name, factor in factors.items():
        out[name] = (out[name] * factor).astype(out[name].dtype)
    return out
```

```python
import math

import numpy as np
import concourse.bass as bass
import concourse.mybir as mybir
from contextlib import ExitStack

F32 = mybir.dt.float32
I32 = mybir.dt.int32
U32 = mybir.dt.uint32
ALU = mybir.AluOpType
ACT = mybir.ActivationFunctionType
AX = mybir.AxisListType

P = 128
NAMES = ["x", "mem", "norm_mix_g", "w_in", "conv_w", "conv_b", "rg_wa", "rg_ba", "rg_wx", "rg_bx",
         "rg_lambda", "s5_lambda_re", "s5_lambda_im", "s5_b_re", "s5_b_im", "s5_c_re", "s5_c_im",
         "s5_d", "s5_log_dt", "s5_glu_w", "s5_glu_b", "w_out", "norm_xa_g", "mem_norm_g", "xa_wq",
         "xa_wkv", "xa_wo", "norm_ffn_g", "router_w", "router_b", "exp_w_gu", "exp_b_gu",
         "exp_w_down", "exp_b_down", "final_norm_g"]


def build(nc, A, out):
    D = A["w_in"].shape[0]
    T = A["x"].shape[1]
    L = T // P
    K = D // P
    CW = A["conv_w"].shape[0]
    CT = A["conv_b"].shape[0] // P
    G, NS = A["s5_lambda_re"].shape
    SC = A["s5_b_re"].shape[2]
    Q = G // 2
    MT = A["mem"].shape[1] // P
    ML = A["mem"].shape[1]
    NH = 4
    HD = D // NH
    E = A["router_w"].shape[1]
    TOPK = 4
    W = 256
    FT = D // P
    ITEMS = (T * TOPK + E * W) // W
    EPS = 1e-6
    HALF = 512
    LIMIT, ALPHA = 7.0, 1.702
    RG_C = 8.0

    ctx = ExitStack()
    with ctx:
        def sb(name, shape, dt=F32):
            return ctx.enter_context(nc.sbuf_tensor(name, shape, dt))

        def sem(name):
            return ctx.enter_context(nc.semaphore(name))

        WA = sb("WA", [P, 16384])
        WB = sb("WB", [P, 8192])
        H = sb("H", [P, L, D])
        XT = sb("XT", [P, K, T])
        YT = sb("YT", [P, K, T])
        ident = sb("ident", [P, P])
        ones = sb("ones", [P, P])
        V = sb("V", [P, 116])
        BGU = sb("BGU", [P, 2 * FT * E])
        BA = sb("BA", [P, CT, P])
        BX = sb("BX", [P, CT, P])
        BG = sb("BG", [P, CT, P])
        CC = sb("CC", [P, 2, Q, SC])
        BB = sb("BB", [P, 2, Q, SC])
        PW = sb("PW", [P, 2, Q, 9])
        sm = sb("sm", [P, 256])
        IOI_ = sb("iota", [P, 32], I32)
        PS = ctx.enter_context(nc.psum_tensor("PS", [P, 8, HALF], F32))

        def wa(off, *dims):
            n = int(np.prod(dims))
            v = WA[:, off:off + n]
            if len(dims) == 1:
                return v
            names = "abcd"[:len(dims)]
            return v.rearrange("p (" + " ".join(names) + ") -> p " + " ".join(names),
                               **{a: d for a, d in zip(names, dims)})

        GM = wa(0, 2, Q, L, SC)
        SR = wa(0, 2, Q, P)
        EM = wa(4096, 2, Q, P)
        MM = wa(8192, L, G * SC)
        RT = wa(12288, 2, Q, P)
        T1 = wa(4096, Q, P)
        T2 = wa(4096 + Q * P, Q, P)
        RW1 = wa(12288, P)
        BGR = wa(12288 + 128, 4, P)
        CRW = wa(12288 + 640, 2, 4, 2, NS)
        BRW = wa(12288 + 1664, 2, Q, SC)
        TMB = wa(12288 + 2692, Q, SC)
        LDT = wa(12288 + 2690, 2)
        SCR = wa(12288 + 2948, 352)
        QV = wa(12288 + 3300, 2, Q, L)
        DB = wa(12288 + 3556, HALF)
        XR0 = wa(0, L, D)
        KT = wa(8192, K, ML)
        VV = wa(10240, MT, D)
        MEM = wa(12288, MT, D)
        MEMT = wa(14336, K, ML)
        PP = wa(0, 2, 2, ML)
        PT = XT[:, :, :].rearrange("p k t -> p (k t)").rearrange("p (h m t) -> p h m t", h=NH, m=MT)
        Hf = H[:, :, :].rearrange("p l d -> p (l d)")
        XRg = Hf[:, 0:T + 4]
        GT = Hf[:, 1028:1028 + 2 * T].rearrange("p (b t) -> p b t", b=2)
        XC, TH, TI, QQ = (Hf[:, 3076 + n * T:3076 + (n + 1) * T] for n in range(4))
        HP = Hf[:, 0:4096].rearrange("p (r q k) -> p r q k", r=2, q=Q)
        YTK = Hf[:, 4096:8192].rearrange("p (l c) -> p l c", l=L)
        TA, TB = Hf[:, 4096:4096 + HALF], Hf[:, 4608:4608 + HALF]
        XTf = XT[:, :, :].rearrange("p k t -> p (k t)")
        SG = XTf[:, 0:2 * HALF].rearrange("p (b n) -> p b n", b=2)
        SQ = XTf[:, 0:2 * D].rearrange("p (b n) -> p b n", b=2)
        UT = XTf[:, 0:4096].rearrange("p (g k) -> p g k", g=G)
        FM = XTf[:, 4096:8192].rearrange("p (r q l c) -> p r q l c", r=2, q=Q, l=L)
        YTf = YT[:, :, :].rearrange("p k t -> p (k t)")
        U = YTf[:, 4096:8192].rearrange("p (g l c) -> p g l c", g=G, l=L)
        KTS = YTf[:, 2048:2048 + HALF]
        WBs = WB[:, :].rearrange("p (s k c) -> p s k c", s=2, k=K)
        RWT = wa(12288, K, E)
        RB = wa(12544, E)
        MTM = wa(15300, L, E)
        LG = wa(12576, L, E)
        TV = wa(12832, L, 8)
        TIu = wa(12896, L, 8).bitcast(U32)
        TIf = wa(12960, L, 8)
        GW = sm[:, 176:208].rearrange("p (l j) -> p l j", l=L)
        IO, IOP = sm[:, 208:240], sm[:, 240:241]
        TOKI, IOI = sm[:, 241:249].bitcast(I32), IOI_[:, :]
        MXT = sm[:, 104:112]
        OH = wa(13088, TOPK, L * E)
        MS = wa(14112, L, E)
        GF = wa(14368, L, E)
        CU = wa(14624, L + 1, E)
        SL = wa(14912, L * E)
        CNT, NTI, PEN, PST = (wa(15168 + 32 * n, E) for n in range(4))
        OHS = YTf[:, 0:1024].rearrange("p (j n) -> p j n", j=TOPK)
        TRI = YTf[:, 1024:1152]
        POSf = YTf[:, 1152:1152 + 32]
        POS = YTf[:, 1184:1216].bitcast(I32)
        ITE = YTf[:, 1224:1227]
        IT1, IT2, IT3 = (YTf[:, 1228 + 32 * n:1260 + 32 * n] for n in range(3))
        ITM = YTf[0:1, 6720:6720 + 3 * P].bitcast(I32)
        POSY = YTf[:, 7104:7136].bitcast(I32)
        CX, IT4 = YTf[:, 7136:7168], YTf[:, 7424:7456]
        SLY = YTf[:, 7168:7424]
        NROW = 2 * (ITEMS + 1)
        TBI = YTf[:, 1580:1708].bitcast(I32)
        TBF = YTf[:, 1708:1836]
        IDX = YTf[:, 1836:1836 + P].bitcast(I32)
        GTT = YTf[:, 1964:1964 + T]
        BDN = YTf[:, 2988:2988 + D]
        IDC = YTf[:, 4012:4014].bitcast(I32)
        BGC = YTf[:, 4014:4014 + 2 * FT]
        GA = YTf[:, 4160:4160 + 2 * W].rearrange("p (b n) -> p b n", b=2)
        SI = YTf[:, 4672:4672 + 2 * W].rearrange("p (b n) -> p b n", b=2)
        UP = YTf[:, 5184:5184 + 2 * W].rearrange("p (b n) -> p b n", b=2)
        FG = YTf[:, 5696:5696 + D]
        XG = XTf[:, 0:2048].rearrange("p (t d) -> p t d", t=2)
        XE = XTf[:, 2048:4096].rearrange("p (k s) -> p k s", k=K)
        HT = XTf[:, 4096:6144].rearrange("p (k s) -> p k s", k=FT)
        YS = XTf[:, 6144:8192].rearrange("p (t d) -> p t d", t=2)
        GUW = WA[:, :].rearrange("p (s h k c) -> p s h k c", s=4, h=2, k=K)
        DNW = WB[:, :].rearrange("p (s k d) -> p s k d", s=4, k=2)
        CB = WA[:, 0:8192].rearrange("p (b j d) -> p b j d", b=2, j=TOPK)

        xn_rows = nc.dram_tensor("xn_rows", (T, D), F32).ap()
        y_rows = nc.dram_tensor("y_rows", (T * TOPK + W, D), F32).ap()
        slot_tok = nc.dram_tensor("slot_tok", (NROW * P, 1), I32).ap()

        V_MIX, V_XA, V_MEM, V_FFN, V_BA, V_BX, V_LAM, V_CW, V_CB = 0, 8, 16, 24, 32, 36, 40, 44, 60
        V_LR, V_LI, V_LD, V_GLB = 64, 80, 96, 112

        order = [("vec",), ("bgu",), ("cre",), ("cim",)]
        order += [("xt", l, h) for l in range(L) for h in range(2)]
        order += [("u", l) for l in range(L)]

        def rg(kind, ct):
            return [(kind, ct, h) for h in range(2)]

        def zz(ct):
            return [("z", ct, w, h) for w in range(2) for h in range(2)]

        order += rg("xr", 0) + rg("g", 0)
        order += [("ktap", b) for b in range(2)] + [("em", n) for n in range(8)]
        for ct in range(CT):
            if ct + 1 < CT:
                order += rg("xr", ct + 1)
            order += zz(ct)
            if ct + 1 < CT:
                order += rg("g", ct + 1)
        order += [("ut", n) for n in range(8)]
        for n in range(4):
            order += [("s", 0, n), ("s", 1, n)]
        order += [("y", n) for n in range(8)]
        order += [("zt", cb, h) for cb in range(CT) for h in range(2)]
        order += [("glu", cb, h) for cb in range(CT) for h in range(2)]
        order += [("wo1", c, l) for c in range(2) for l in range(L)]
        order += [("mt", m, h) for m in range(MT) for h in range(2)]
        order += [("kk", j) for j in range(K)] + [("vv", c, m) for c in range(2) for m in range(MT)]
        order += [("xt2", l, h) for l in range(L) for h in range(2)]
        order += [("q", j, h) for j in range(K) for h in range(2)]
        att = [(l, hp) for l in range(L) for hp in range(2)]
        LEAD = 3
        for n in range(len(att) + LEAD):
            if n < len(att):
                order.append(("sc",) + att[n])
            if n >= LEAD:
                order.append(("pt",) + att[n - LEAD])
        order += [("ot", h, d, f) for h in range(NH) for d in range(2) for f in range(2)]
        order += [("wo2", c, l) for c in range(2) for l in range(L)]
        order += [("xt3", l, h) for l in range(L) for h in range(2)]
        order += [("rt",), ("rank",), ("cnt",), ("itm",), ("gft", 0), ("gft", 1)]
        order += [("bd", l, c) for l in range(L) for c in range(2)]
        order += [("idx",)]
        number = {u: n for n, u in enumerate(order)}
        filled = [sem(f"bank{b}_filled") for b in range(8)]
        emptied = [sem(f"bank{b}_emptied") for b in range(8)]

        def bank(u):
            return PS[:, number[u] % 8, :]

        def wait_filled(eng, u):
            eng.wait_ge(filled[number[u] % 8], number[u] // 8 + 1)

        def emptied_by(u):
            return emptied[number[u] % 8]

        dve_step, act_step, pool_step = sem("dve_step"), sem("act_step"), sem("pool_step")
        steps = {}

        def link(eng, ins, s):
            steps[s.name] = steps.get(s.name, 0) + 1
            ins.then_inc(s, 1)
            eng.wait_ge(s, steps[s.name])

        def evac(eng, ins, u, own=False):
            s = emptied[number[u] % 8]
            ins.then_inc(s, 1)
            if own:
                eng.wait_ge(s, number[u] // 8 + 1)

        def units_read(eng, kind):
            for b in range(8):
                last = max((n for u, n in number.items() if u[0] == kind and n % 8 == b), default=None)
                if last is not None:
                    eng.wait_ge(emptied[b], last // 8 + 1)

        x_in = [sem(f"x_in{n}") for n in range(2)]
        vec_in, par_in, blk_in, mem_in = sem("vec_in"), sem("par_in"), sem("blk_in"), sem("mem_in")
        x_again, d_in, rt_in, zero_out = sem("x_again"), sem("d_in"), sem("rt_in"), sem("zero_out")
        w_in_s = [sem(f"wslot{s}_in") for s in range(2)]
        consts, ldt_ready, zeroed, eps_done = sem("consts"), sem("ldt_ready"), sem("zeroed"), sem("eps_done")
        ssq_done = [sem(f"ssq{n}_done") for n in range(5)]
        rstd_done = [sem(f"rstd{n}_done") for n in range(5)]
        xn_done = [sem(f"xn{n}_done") for n in range(4)]
        v_done, dt_done, ang_done, trig_done, rgc_done = (
            sem("v_done"), sem("dt_done"), sem("ang_done"), sem("trig_done"), sem("rgc_done"))
        bb_done, g_done, rot_done, f_done = sem("bb_done"), sem("g_done"), sem("rot_done"), sem("f_done")
        kts_done, mm_in, hp_done = sem("kts_done"), sem("mm_in"), sem("hp_done")
        glu_done, db_done, iota_done, y_zero = sem("glu_done"), sem("db_done"), sem("iota_done"), sem("y_zero")
        xr_zero, xc_done, rg_tp, rg_q, rg_sq, rg_done = (
            sem("xr_zero"), sem("xc_done"), sem("rg_tp"), sem("rg_q"), sem("rg_sq"), sem("rg_done"))
        h1_done, h2_done = sem("h1_done"), sem("h2_done")
        mx_done, exp_done, pn_done = sem("mx_done"), sem("exp_done"), sem("pn_done")
        xn_out, gexp_in, gexp_done, gf_done = sem("xn_out"), sem("gexp_in"), sem("gexp_done"), sem("gf_done")
        ms_done, pos_done, itm_done, ite_done = sem("ms_done"), sem("pos_done"), sem("itm_done"), sem("ite_done")
        scat, tb_in, tbf_done, idx_done = sem("scat"), sem("tb_in"), sem("tbf_done"), sem("idx_done")
        bdn_in, tri_done, fg_in, h3_done = sem("bdn_in"), sem("tri_done"), sem("fg_in"), sem("h3_done")
        gu_in = [sem(f"gu{s}_in") for s in range(4)]
        dn_in = [sem(f"dn{s}_in") for s in range(4)]
        xg_in, xe_filled, xe_done, idc_done = sem("xg_in"), sem("xe_filled"), sem("xe_done"), sem("idc_done")
        gb_filled, gb_free, ga_done, si_done, ht_done = (
            sem("gb_filled"), sem("gb_free"), sem("ga_done"), sem("si_done"), sem("ht_done"))
        dn_used, y_done, y_out, bgc_done, ffn_step = (
            sem("dn_used"), sem("y_done"), sem("y_out"), sem("bgc_done"), sem("ffn_step"))
        gather_go, ys_free = sem("gather_go"), sem("ys_free")
        cb_in = [sem(f"cb{b}_in") for b in range(2)]
        comb_done, out_ready, out_sent = sem("comb_done"), sem("out_ready"), sem("out_sent")

        def cols(name, c0):
            return A[name][:, c0:c0 + HALF].rearrange("(k p) c -> p k c", p=P)

        RGC = CT * P
        chunks = [("u", cols("w_in", 2 * RGC)), ("xr", cols("w_in", RGC)), ("g", cols("w_in", 0))]
        chunks += [(("o1", c), cols("w_out", c * HALF)) for c in range(2)]
        chunks += [(("kv", c), cols("xa_wkv", c * HALF)) for c in range(4)]
        chunks += [(("q", c), cols("xa_wq", c * HALF)) for c in range(2)]
        chunks += [(("o2", c), cols("xa_wo", c * HALF)) for c in range(2)]
        chunk_no = {name: n for n, (name, _) in enumerate(chunks)}

        def wslot(name):
            return WBs[:, chunk_no[name] % 2, :, :]

        block = ctx.enter_context(nc.Block())

        x_tok = A["x"].rearrange("b (p l) d -> p (b l) d", l=L)
        o_tok = out.rearrange("b (p l) d -> p (b l) d", l=L)

        def by_width(eng, n_i, item):
            with eng.If(n_i > 0):
                with eng.If(n_i > P):
                    with eng.If(n_i > 192):
                        item(W)
                    with eng.Else():
                        with eng.If(n_i > 160):
                            item(192)
                        with eng.Else():
                            item(160)
                with eng.Else():
                    item(P)

        def item_tokens(eng, i):
            return eng.value_load(ITM[0:1, bass.ds(i + P, 1)], min_val=0, max_val=W)

        def item_expert(eng, i):
            return eng.value_load(ITM[0:1, bass.ds(i, 1)], min_val=0, max_val=E - 1)

        @block.sync
        def _(sp):
            for n in range(2):
                sp.dma_start(H[:, 4 * n:4 * n + 4, :], x_tok[:, 4 * n:4 * n + 4, :]).then_inc(x_in[n], 16)
            sp.dma_start(wslot("u"), chunks[0][1]).then_inc(w_in_s[0], 16)
            sp.dma_start(wslot("xr"), chunks[1][1]).then_inc(w_in_s[1], 16)
            last_unit = {"u": ("u", L - 1), "xr": ("xr", CT - 1, 1), "g": ("g", CT - 1, 1)}
            for c in range(2):
                last_unit[("o1", c)] = ("wo1", c, L - 1)
                last_unit[("o2", c)] = ("wo2", c, L - 1)
                last_unit[("kv", c)] = ("kk", 4 * c + 3)
                last_unit[("kv", 2 + c)] = ("vv", c, MT - 1)
                last_unit[("q", c)] = ("q", 4 * c + 3, 1)
            for n in range(2, len(chunks)):
                wait_filled(sp, last_unit[chunks[n - 2][0]])
                sp.dma_start(WBs[:, n % 2, :, :], chunks[n][1]).then_inc(w_in_s[n % 2], 16)
                if n == 4:
                    wait_filled(sp, ("y", 7))
                    sp.dma_start(XR0, x_tok).then_inc(x_again, 16)
                    sp.dma_start(MEM, A["mem"].rearrange("b (m p) d -> p (b m) d", p=P)).then_inc(mem_in, 16)
            wait_filled(sp, ("ot", NH - 1, 1, 1))
            sp.dma_start(RWT, A["router_w"].rearrange("(k p) e -> p k e", p=P)).then_inc(rt_in, 16)
            sp.dma_start(RB, A["router_b"].partition_broadcast(P)).then_inc(rt_in, 16)
            for l in range(L):
                sp.wait_ge(xn_done[3], l + 1)
                sp.dma_start(xn_rows.rearrange("(p l) d -> p l d", l=L)[:, l, :], XR0[:, l, :]).then_inc(xn_out, 16)
            sp.dma_start(BDN[0:E, :], A["exp_b_down"]).then_inc(bdn_in, 16)
            sp.dma_start(FG, A["final_norm_g"].partition_broadcast(P)).then_inc(fg_in, 16)
            sp.wait_ge(scat, 16 * TOPK * L)
            sp.dma_start(TBI[0:NROW, :], slot_tok.rearrange("(r p) o -> r (p o)", p=P)).then_inc(tb_in, 16)

            gu_v = A["exp_w_gu"].rearrange("e (k p) (h c) -> p e h k c", p=P, h=2)
            dn_v = A["exp_w_down"].rearrange("e (k p) d -> p e k d", p=P)
            sp.wait_ge(itm_done, 1)
            with sp.Fori(0, ITEMS) as i:
                with sp.If(item_tokens(sp, i) > 0):
                    e_i = item_expert(sp, i)
                    for s in range(4):
                        sp.wait_ge(gb_filled, 8 * i + 2 * s + 2)
                        for h in range(2):
                            sp.dma_start(GUW[:, s, h, :, :],
                                         gu_v[:, bass.ds(e_i, 1), h, :, s * 256:(s + 1) * 256]
                                         .rearrange("p e k c -> p (e k) c")).then_inc(gu_in[s], 16)
                    for s in range(4):
                        sp.wait_ge(dn_used, 4 * i + s + 1)
                        sp.dma_start(DNW[:, s, :, :],
                                     dn_v[:, bass.ds(e_i, 1), 2 * s:2 * s + 2, :]
                                     .rearrange("p e k d -> p (e k) d")).then_inc(dn_in[s], 16)
            for l in range(L):
                sp.wait_ge(out_ready, l + 1)
                sp.dma_start(o_tok[:, l, :], H[:, l, :]).then_inc(out_sent, 16)
            sp.wait_ge(out_sent, 16 * L)

        @block.tensor
        def _(pe):
            def begin(u):
                n = number[u]
                if n >= 8:
                    pe.wait_ge(emptied[n % 8], n // 8)
                return PS[:, n % 8, :]

            def end(u, ins):
                ins.then_inc(filled[number[u] % 8], 1)

            def weights(name):
                n = chunk_no[name]
                pe.wait_ge(w_in_s[n % 2], 16 * (n // 2 + 1))
                return WBs[:, n % 2, :, :]

            def mm(o, a, b, k, n):
                return nc.tensor.matmul(o, a, b, start=(k == 0), stop=(k == n - 1))

            pe.wait_ge(consts, 2)
            pe.wait_ge(vec_in, 16 * 13)
            pe.wait_ge(ldt_ready, 1)
            o = begin(("vec",))
            end(("vec",), nc.tensor.transpose(o[:, 0:116], RW1[0:116, :], ident[0:116, 0:116]))
            pe.wait_ge(par_in, 16 * 10)
            o = begin(("bgu",))
            for r in range(4):
                ins = nc.tensor.transpose(o[:, r * P:(r + 1) * P], BGR[:, r, :], ident[:])
            end(("bgu",), ins)
            for w, u in enumerate((("cre",), ("cim",))):
                o = begin(u)
                for r in range(4):
                    ins = nc.tensor.transpose(o[:, r * P:(r + 1) * P],
                                              CRW[:, w, r, :, :].rearrange("p a b -> p (a b)"), ident[:])
                end(u, ins)

            def transposes(kind, norm, src):
                for l in range(L):
                    pe.wait_ge(xn_done[norm], l + 1)
                    for h in range(2):
                        o = begin((kind, l, h))
                        for k in range(4):
                            c = (4 * h + k) * P
                            ins = nc.tensor.transpose(o[:, k * P:(k + 1) * P], src[:, l, c:c + P], ident[:])
                        end((kind, l, h), ins)

            transposes("xt", 0, YT)
            w = weights("u")
            units_read(pe, "xt")
            for l in range(L):
                o = begin(("u", l))
                for k in range(K):
                    ins = mm(o, XT[:, k, l * P:(l + 1) * P], w[:, k, :], k, K)
                end(("u", l), ins)

            def proj(kind, ct):
                w = weights(kind)
                for h in range(2):
                    o = begin((kind, ct, h))
                    for k in range(K):
                        ins = mm(o, w[:, k, ct * P:(ct + 1) * P], XT[:, k, h * HALF:(h + 1) * HALF], k, K)
                    end((kind, ct, h), ins)

            def gates(ct):
                pe.wait_ge(xc_done, ct + 1)
                for w2, wt in enumerate((BA, BX)):
                    for h in range(2):
                        o = begin(("z", ct, w2, h))
                        end(("z", ct, w2, h), mm(o, wt[:, ct, :], XC[:, h * HALF:(h + 1) * HALF], 0, 1))

            proj("xr", 0)
            proj("g", 0)
            pe.wait_ge(g_done, 1)
            for b in range(2):
                r = slice(NS * b, NS * b + NS)
                o = begin(("ktap", b))
                for q in range(Q):
                    for w2 in range(2):
                        ins = mm(o[:, q * SC:(q + 1) * SC],
                                 GM[r, w2, q, :, :].rearrange("p a b -> p (a b)"), CC[r, w2, q, :], w2, 2)
                end(("ktap", b), ins)
            for n in range(8):
                o = begin(("em", n))
                for j in range(4):
                    w2, q = divmod(4 * n + j, Q)
                    ins = nc.tensor.transpose(o[:, j * P:(j + 1) * P],
                                              GM[:, w2, q, :, :].rearrange("p a b -> p (a b)"), ident[:])
                end(("em", n), ins)
            pe.wait_ge(blk_in, 16 * 12)
            for ct in range(CT):
                if ct + 1 < CT:
                    proj("xr", ct + 1)
                gates(ct)
                if ct + 1 < CT:
                    proj("g", ct + 1)

            units_read(pe, "u")
            for n in range(8):
                o = begin(("ut", n))
                for j in range(4):
                    g = 4 * n + j
                    ins = nc.tensor.transpose(o[:, j * P:(j + 1) * P], U[:, g, :, :].rearrange("p a b -> p (a b)"), ident[:])
                end(("ut", n), ins)
            units_read(pe, "em")
            units_read(pe, "ut")
            for n in range(4):
                for w2 in range(2):
                    o = begin(("s", w2, n))
                    for j in range(4):
                        q = 4 * n + j
                        for b in range(2):
                            r = slice(NS * b, NS * b + NS)
                            ins = mm(o[r, j * P:(j + 1) * P], EM[:, w2, q, r], UT[:, 2 * q + b, :], 0, 1)
                    end(("s", w2, n), ins)
            pe.wait_ge(mm_in, 16 * L)
            pe.wait_ge(hp_done, 1)
            pe.wait_ge(f_done, 1)
            for n in range(8):
                o = begin(("y", n))
                for j in range(4):
                    g = 8 * (n // 2) + 2 * j + n % 2
                    r = slice(NS * (g % 2), NS * (g % 2) + NS)
                    oo = o[:, j * P:(j + 1) * P]
                    mm(oo, UT[:, g, :], MM[:, :, g * SC:(g + 1) * SC], 0, 3)
                    for w2 in range(2):
                        ins = mm(oo, HP[r, w2, g // 2, :],
                                 FM[r, w2, g // 2, :, :].rearrange("p a b -> p (a b)"), w2 + 1, 3)
                end(("y", n), ins)
            units_read(pe, "y")
            for cb in range(CT):
                for h in range(2):
                    o = begin(("zt", cb, h))
                    for j in range(4):
                        ins = nc.tensor.transpose(o[:, j * P:(j + 1) * P],
                                                  YTK[:, 4 * h + j, cb * P:(cb + 1) * P], ident[:])
                    end(("zt", cb, h), ins)
            units_read(pe, "zt")
            for cb in range(CT):
                for h in range(2):
                    o = begin(("glu", cb, h))
                    end(("glu", cb, h), mm(o, BG[:, cb, :], YT[:, CT + cb, h * HALF:(h + 1) * HALF], 0, 1))
            pe.wait_ge(glu_done, 2 * CT)
            pe.wait_ge(rg_done, CT)

            def out_proj(kind, name):
                for c in range(2):
                    w = weights((name, c))
                    for l in range(L):
                        o = begin((kind, c, l))
                        for k in range(K):
                            ins = mm(o, YT[:, k, l * P:(l + 1) * P], w[:, k, :], k, K)
                        end((kind, c, l), ins)

            out_proj("wo1", "o1")
            for m in range(MT):
                pe.wait_ge(xn_done[1], m + 1)
                for h in range(2):
                    o = begin(("mt", m, h))
                    for k in range(4):
                        c = (4 * h + k) * P
                        ins = nc.tensor.transpose(o[:, k * P:(k + 1) * P], MEM[:, m, c:c + P], ident[:])
                    end(("mt", m, h), ins)
            units_read(pe, "mt")
            for c in range(2):
                w = weights(("kv", c))
                for j in range(4):
                    o = begin(("kk", 4 * c + j))
                    for k in range(K):
                        ins = mm(o[:, 0:ML], w[:, k, j * P:(j + 1) * P], MEMT[:, k, :], k, K)
                    end(("kk", 4 * c + j), ins)
            for c in range(2):
                w = weights(("kv", 2 + c))
                for m in range(MT):
                    o = begin(("vv", c, m))
                    for k in range(K):
                        ins = mm(o, MEMT[:, k, m * P:(m + 1) * P], w[:, k, :], k, K)
                    end(("vv", c, m), ins)
            transposes("xt2", 2, XR0)
            units_read(pe, "xt2")
            for c in range(2):
                w = weights(("q", c))
                for j in range(4):
                    for h in range(2):
                        u = ("q", 4 * c + j, h)
                        o = begin(u)
                        for k in range(K):
                            ins = mm(o, w[:, k, j * P:(j + 1) * P], XT[:, k, h * HALF:(h + 1) * HALF], k, K)
                        end(u, ins)
            for kind in ("q", "kk", "vv"):
                units_read(pe, kind)
            for n in range(len(att) + LEAD):
                if n < len(att):
                    l, hp = att[n]
                    o = begin(("sc", l, hp))
                    for hh in range(2):
                        for d in range(2):
                            k = 2 * (2 * hp + hh) + d
                            ins = mm(o[:, hh * ML:(hh + 1) * ML], YT[:, k, l * P:(l + 1) * P], KT[:, k, :], d, 2)
                    end(("sc", l, hp), ins)
                if n >= LEAD:
                    l, hp = att[n - LEAD]
                    pe.wait_ge(pn_done, n - LEAD + 1)
                    o = begin(("pt", l, hp))
                    for hh in range(2):
                        for m in range(MT):
                            ins = nc.tensor.transpose(o[:, (2 * hh + m) * P:(2 * hh + m + 1) * P],
                                                      PP[:, (n - LEAD) % 2, hh, m * P:(m + 1) * P], ident[:])
                    end(("pt", l, hp), ins)
            units_read(pe, "pt")
            for h in range(NH):
                for d in range(2):
                    for f in range(2):
                        o = begin(("ot", h, d, f))
                        for m in range(MT):
                            c = h * HD + d * P
                            ins = mm(o, VV[:, m, c:c + P], PT[:, h, m, f * HALF:(f + 1) * HALF], m, MT)
                        end(("ot", h, d, f), ins)
            units_read(pe, "ot")
            out_proj("wo2", "o2")
            transposes("xt3", 3, XR0)
            units_read(pe, "xt3")
            pe.wait_ge(rt_in, 32)
            o = begin(("rt",))
            for l in range(L):
                for k in range(K):
                    ins = mm(o[:, l * E:(l + 1) * E], XT[:, k, l * P:(l + 1) * P], RWT[:, k, :], k, K)
            end(("rt",), ins)
            pe.wait_ge(ms_done, 1)
            pe.wait_ge(tri_done, 1)
            o = begin(("rank",))
            mm(o[:, 0:L * E], TRI, MS.rearrange("p a b -> p (a b)"), 0, 2)
            end(("rank",), mm(o[:, 0:L * E], ones[:], CU[:, 0:L, :].rearrange("p a b -> p (a b)"), 1, 2))
            o = begin(("cnt",))
            end(("cnt",), mm(o[:, 0:E], ones[:], CU[:, L, :], 0, 1))
            pe.wait_ge(ite_done, 1)
            o = begin(("itm",))
            mm(o[0:1, 0:P], ITE[:, 0:1], ident[:], 0, 1)
            mm(o[0:1, P:2 * P], ITE[:, 1:2], ident[:], 0, 1)
            end(("itm",), mm(o[0:1, 2 * P:3 * P], ITE[:, 2:3], ident[:], 0, 1))
            pe.wait_ge(gf_done, 1)
            for h in range(2):
                o = begin(("gft", h))
                for j in range(4):
                    ins = nc.tensor.transpose(o[0:E, j * P:(j + 1) * P], GF[:, 4 * h + j, :], ident[:])
                end(("gft", h), ins)
            pe.wait_ge(bdn_in, 16)
            units_read(pe, "gft")
            for l in range(L):
                for c in range(2):
                    o = begin(("bd", l, c))
                    end(("bd", l, c), mm(o, GTT[0:E, l * P:(l + 1) * P], BDN[0:E, c * HALF:(c + 1) * HALF], 0, 1))
            pe.wait_ge(tbf_done, 1)
            o = begin(("idx",))
            end(("idx",), nc.tensor.transpose(o[:, 0:NROW], TBF[0:NROW, :], ident[0:NROW, 0:NROW]))
            for b in range(8):
                last = max(n for n in number.values() if n % 8 == b)
                pe.wait_ge(emptied[b], last // 8 + 1)
            pe.sem_inc(gb_filled, 8)
            pe.sem_inc(dn_used, 4)
            pe.wait_ge(itm_done, 1)

            def item_transposes():
                for kp in range(K // 2):
                    o = PS[:, 2 + kp % 2, :].rearrange("p (k s) -> p k s", k=2)
                    for kk in range(2):
                        for t in range(2):
                            c = (2 * kp + kk) * P
                            ins = nc.tensor.transpose(o[:, kk, t * P:(t + 1) * P], XG[:, t, c:c + P], ident[:])
                    yield kp, ins

            pe.wait_ge(xg_in, 32)
            for kp, ins in item_transposes():
                ins.then_inc(xe_filled, 1)
                pe.wait_ge(xe_done, kp + 1)
            with pe.Fori(0, ITEMS) as i:
                n_i = item_tokens(pe, i)

                def item(n):
                    for f in range(FT):
                        s, f2 = divmod(f, 2)
                        if f2 == 0:
                            pe.wait_ge(gu_in[s], 32 * i + 32)
                        pe.wait_ge(gb_free, 8 * i + f + 1)
                        for hh in range(2):
                            for k in range(K):
                                ins = mm(PS[:, f % 2, hh * W:hh * W + n],
                                         GUW[:, s, hh, k, f2 * P:(f2 + 1) * P], XE[:, k, 0:n], k, K)
                        ins.then_inc(gb_filled, 1)
                    pe.wait_ge(xg_in, 32 * i + 64)
                    for kp, ins in item_transposes():
                        ins.then_inc(xe_filled, 1)
                        if kp >= 1:
                            pe.wait_ge(xe_done, 4 * i + 4 + kp)
                    pe.wait_ge(y_done, i + 1)
                    pe.wait_ge(ht_done, 8 * i + 8)
                    for s in range(4):
                        pe.wait_ge(dn_in[s], 16 * i + 16)
                        for k2 in range(2):
                            k = 2 * s + k2
                            for t in range((n + P - 1) // P):
                                m = min(P, n - t * P)
                                for c in range(2):
                                    ins = mm(PS[0:m, 4 + 2 * t + c, :], HT[:, k, t * P:t * P + m],
                                             DNW[:, s, k2, c * HALF:(c + 1) * HALF], k, FT)
                        ins.then_inc(dn_used, 1)
                    pe.wait_ge(xe_done, 4 * i + 8)

                by_width(pe, n_i, item)

        @block.scalar
        def _(act):
            def a(dst, src, func, s=act_step, **kw):
                link(act, nc.scalar.activation(dst, src, func, **kw), s)

            def copy_unit(u, dst):
                wait_filled(act, u)
                evac(act, nc.scalar.copy(dst, bank(u)), u)

            bgu_rows = A["exp_b_gu"].rearrange("e (f p) -> (e f) p", p=P)
            for t in range(4):
                act.dma_start(BGR[:, t, :], bgu_rows[t * P:(t + 1) * P, :]).then_inc(par_in, 16)
            rows = [("norm_mix_g", V_MIX), ("norm_xa_g", V_XA), ("mem_norm_g", V_MEM), ("norm_ffn_g", V_FFN),
                    ("rg_ba", V_BA), ("rg_bx", V_BX), ("rg_lambda", V_LAM), ("conv_b", V_CB), ("s5_glu_b", V_GLB)]
            for name, r in rows:
                n = A[name].shape[0] // P
                act.dma_start(RW1[r:r + n, :], A[name].rearrange("(n p) -> n p", p=P)).then_inc(vec_in, 16)
            act.dma_start(RW1[V_CW:V_CW + CW * CT, :],
                          A["conv_w"].rearrange("k (n p) -> (k n) p", p=P)).then_inc(vec_in, 16)
            for name, r in (("s5_lambda_re", V_LR), ("s5_lambda_im", V_LI)):
                act.dma_start(RW1[r:r + Q, :], A[name].rearrange("(q b) n -> q (b n)", b=2)).then_inc(vec_in, 16)
            act.dma_start(LDT[V_LD:V_LD + Q, :], A["s5_log_dt"].rearrange("(q b) -> q b", b=2)).then_inc(vec_in, 16)
            for w, name in enumerate(("s5_c_re", "s5_c_im")):
                for b in range(2):
                    act.dma_start(CRW[:, w, :, b, :],
                                  A[name].rearrange("(t g) c n -> (g c) t n", t=4)).then_inc(par_in, 16)
            for w, name in enumerate(("s5_b_re", "s5_b_im")):
                act.dma_start(BRW[:, w, :, :], A[name].rearrange("(q b) n c -> (b n) q c", b=2)).then_inc(par_in, 16)
            act.dma_start(DB, A["s5_d"].partition_broadcast(P)).then_inc(d_in, 16)

            def norm(n, l, src, dst, c0, count=1):
                a(dst, src, ACT.Square, accum_out=sm[:, c0:c0 + 1])
                a(sm[:, c0 + 8:c0 + 9], sm[:, c0:c0 + 1], ACT.Sqrt, bias=sm[:, 127:128], scale=1.0 / D, s=ssq_done[n])
                act.wait_ge(rstd_done[n], l + 1)
                a(dst, src, ACT.Copy, scale=sm[:, c0 + 16:c0 + 17], s=xn_done[n])

            act.wait_ge(eps_done, 1)
            for l in range(L):
                if l % 4 == 0:
                    act.wait_ge(x_in[l // 4], 16)
                norm(0, l, H[:, l, :], YT[:, l, :], l)
            act.wait_ge(zeroed, 3)
            for t, name in ((BA, "rg_wa"), (BX, "rg_wx")):
                for b in range(2):
                    act.dma_start(t[64 * b:64 * b + 64, :, 64 * b:64 * b + 64],
                                  A[name].rearrange("(c b) i j -> b i c j", b=2)[b]).then_inc(blk_in, 16)
            for b in range(8):
                act.dma_start(BG[SC * b:SC * (b + 1), :, SC * b:SC * (b + 1)],
                              A["s5_glu_w"].rearrange("(c b) i j -> b i c j", b=8)[b]).then_inc(blk_in, 16)
            act.wait_ge(v_done, 1)
            a(sm[:, 24:40], V[:, V_LD:V_LD + Q], ACT.Exp, s=dt_done)
            act.wait_ge(ang_done, 3)
            a(sm[:, 40:56], sm[:, 40:56], ACT.Exp)
            a(sm[:, 88:92], sm[:, 88:92], ACT.Exp)
            a(sm[:, 56:72], sm[:, 56:72], ACT.Sin)
            a(sm[:, 72:88], sm[:, 72:88], ACT.Sin, s=trig_done)
            for l in range(L):
                wait_filled(act, ("u", l))
                evac(act, nc.scalar.copy(U[:, :, l, :], bank(("u", l)).rearrange("p (g c) -> p g c", g=G)), ("u", l))

            def xr(ct):
                act.wait_ge(xr_zero, 1)
                if ct:
                    act.wait_ge(xc_done, ct)
                for h in range(2):
                    u = ("xr", ct, h)
                    wait_filled(act, u)
                    dst = XRg[:, 3:3 + T].rearrange("p (k l) -> p l k", l=L)[:, 4 * h:4 * h + 4, :]
                    evac(act, nc.scalar.copy(dst, bank(u).rearrange("p (l k) -> p l k", l=4)), u)

            def gate(ct):
                if ct >= 2:
                    act.wait_ge(rg_done, ct - 1)
                for h in range(2):
                    u = ("g", ct, h)
                    wait_filled(act, u)
                    dst = GT[:, ct % 2, :].rearrange("p (k l) -> p l k", l=L)[:, 4 * h:4 * h + 4, :]
                    evac(act, nc.scalar.activation(dst, bank(u).rearrange("p (l k) -> p l k", l=4),
                                                   ACT.Gelu_apprx_tanh), u)

            def rg_gates(ct):
                if ct:
                    act.wait_ge(rg_done, ct)
                for w, (t, c) in enumerate(((TH, 0), (TI, 4))):
                    for h in range(2):
                        u = ("z", ct, w, h)
                        wait_filled(act, u)
                        evac(act, nc.scalar.activation(t[:, h * HALF:(h + 1) * HALF], bank(u), ACT.Tanh, scale=0.5,
                                                       bias=sm[:, 92 + c + ct:93 + c + ct]), u, own=True)
                a(TH, TH, ACT.Tanh, bias=sm[:, 100 + ct:101 + ct], scale=sm[:, 100 + ct:101 + ct], s=rg_tp)
                act.wait_ge(rg_q, ct + 1)
                a(TH, TH, ACT.Sqrt, s=rg_sq)

            xr(0)
            gate(0)
            for n in range(8):
                copy_unit(("em", n), EM.rearrange("p a b c -> p (a b c)")[:, n * HALF:(n + 1) * HALF])
            act.wait_ge(rgc_done, 1)
            for ct in range(CT):
                if ct + 1 < CT:
                    xr(ct + 1)
                rg_gates(ct)
                if ct + 1 < CT:
                    gate(ct + 1)
            for n in range(8):
                copy_unit(("ut", n), XTf[:, n * HALF:(n + 1) * HALF])
            for n in range(8):
                u = ("y", n)
                wait_filled(act, u)
                dst = YTK[:, :, (n // 2) * 128:(n // 2) * 128 + 128].rearrange("p l (g b c) -> p b g l c", g=4, b=2)
                evac(act, nc.scalar.copy(dst[:, n % 2], bank(u).rearrange("p (g l c) -> p g l c", g=4, l=L)), u)
            for cb in range(CT):
                for h in range(2):
                    u = ("zt", cb, h)
                    wait_filled(act, u)
                    evac(act, nc.scalar.activation(YT[:, CT + cb, h * HALF:(h + 1) * HALF], bank(u),
                                                   ACT.Gelu_apprx_tanh), u)
            for n in range(2 * CT):
                cb, h = divmod(n, 2)
                u = ("glu", cb, h)
                wait_filled(act, u)
                if n >= 2:
                    act.wait_ge(glu_done, n - 1)
                evac(act, nc.scalar.activation(SG[:, n % 2, :], bank(u), ACT.Sigmoid,
                                               bias=V[:, V_GLB + cb:V_GLB + cb + 1]), u)
            act.wait_ge(mem_in, 16)
            for m in range(MT):
                a(MEMT.rearrange("p k s -> p (k s)")[:, m * D:(m + 1) * D], MEM[:, m, :], ACT.Square,
                  accum_out=sm[:, 104 + m:105 + m])
                a(sm[:, 112 + m:113 + m], sm[:, 104 + m:105 + m], ACT.Sqrt, bias=sm[:, 127:128], scale=1.0 / D,
                  s=ssq_done[1])
                act.wait_ge(rstd_done[1], m + 1)
                a(MEM[:, m, :], MEM[:, m, :], ACT.Copy, scale=sm[:, 120 + m:121 + m], s=xn_done[1])
            for j in range(K):
                u = ("kk", j)
                wait_filled(act, u)
                evac(act, nc.scalar.copy(KT[:, j, :], bank(u)[:, 0:ML]), u)
            for c in range(2):
                for m in range(MT):
                    copy_unit(("vv", c, m), VV[:, m, c * HALF:(c + 1) * HALF])
            for l in range(L):
                act.wait_ge(h1_done, L + l + 1)
                norm(2, l, H[:, l, :], XR0[:, l, :], l)
            for j in range(K):
                for h in range(2):
                    copy_unit(("q", j, h), YT[:, j, h * HALF:(h + 1) * HALF])
            for n, (l, hp) in enumerate(att):
                u = ("sc", l, hp)
                act.wait_ge(mx_done, n + 1)
                if n >= 2:
                    wait_filled(act, ("pt",) + att[n - 2])
                b = n % 2
                for hh in range(2):
                    ins = nc.scalar.activation(PP[:, b, hh, :], bank(u)[:, hh * ML:(hh + 1) * ML], ACT.Exp,
                                               bias=sm[:, 24 + 2 * b + hh:25 + 2 * b + hh], scale=HD ** -0.5,
                                               accum_out=sm[:, 28 + 2 * b + hh:29 + 2 * b + hh])
                    if hh == 0:
                        ins.then_inc(exp_done, 1)
                evac(act, ins, u, own=True)
                act.sem_inc(exp_done, 1)
            for h in range(NH):
                for d in range(2):
                    for f in range(2):
                        copy_unit(("ot", h, d, f), YT[:, 2 * h + d, f * HALF:(f + 1) * HALF])
            for l in range(L):
                act.wait_ge(h2_done, L + l + 1)
                norm(3, l, H[:, l, :], XR0[:, l, :], l)
            act.wait_ge(gexp_in, 1)
            a(GW, GW, ACT.Exp, s=gexp_done)
            for h in range(2):
                u = ("gft", h)
                wait_filled(act, u)
                evac(act, nc.scalar.copy(GTT[0:E, h * HALF:(h + 1) * HALF], bank(u)[0:E, :]), u)

            def pair(kp, count):
                act.wait_ge(xe_filled, count)
                o = PS[:, 2 + kp % 2, :].rearrange("p (k s) -> p k s", k=2)
                for kk in range(2):
                    k = 2 * kp + kk
                    ins = nc.scalar.activation(XE[:, k, :], o[:, kk, :], ACT.Copy, scale=V[:, V_FFN + k:V_FFN + k + 1])
                ins.then_inc(xe_done, 1)

            act.wait_ge(itm_done, 1)
            for kp in range(4):
                pair(kp, kp + 1)
            act.sem_inc(y_done, 1)
            with act.Fori(0, ITEMS) as i:
                n_i = item_tokens(act, i)

                def item(n):
                    for f in range(FT):
                        act.wait_ge(ga_done, 8 * i + f + 1)
                        nc.scalar.activation(SI[:, f % 2, 0:n], GA[:, f % 2, 0:n], ACT.Sigmoid, scale=ALPHA) \
                            .then_inc(si_done, 1)
                    for kp in range(4):
                        pair(kp, 4 * i + kp + 5)
                    act.wait_ge(dn_used, 4 * i + 8)
                    act.wait_ge(ys_free, i + 1)
                    for t in range((n + P - 1) // P):
                        m = min(P, n - t * P)
                        ins = nc.scalar.copy(YS[0:m, t, :],
                                             PS[0:m, 4 + 2 * t:6 + 2 * t, :].rearrange("p a b -> p (a b)"))
                    ins.then_inc(y_done, 1)

                by_width(act, n_i, item)
            for l in range(L):
                act.wait_ge(comb_done, l + 1)
                a(SQ[:, l % 2, :], H[:, l, :], ACT.Square, accum_out=sm[:, l:l + 1])
                a(sm[:, l + 8:l + 9], sm[:, l:l + 1], ACT.Sqrt, bias=sm[:, 127:128], scale=1.0 / D, s=ssq_done[4])

        @block.vector
        def _(dve):
            v = nc.vector

            def d(ins, s=dve_step):
                link(dve, ins, s)

            def tt(o, x, y, op, s=dve_step):
                d(v.tensor_tensor(o, x, y, op), s)

            def ts(o, x, c1, c2, op0, op1=ALU.bypass, s=dve_step):
                d(v.tensor_scalar(o, x, c1, c2, op0, op1) if c2 is not None else v.tensor_scalar(o, x, c1, None, op0), s)

            def stt(o, x, c, y, op0, op1, s=dve_step):
                d(v.scalar_tensor_tensor(out=o, in0=x, scalar=c, in1=y, op0=op0, op1=op1), s)

            mul, add, sub = ALU.mult, ALU.add, ALU.subtract
            d(v.memset(sm[:, 127:128], EPS), eps_done)
            dve.wait_ge(vec_in, 16 * 13)
            d(v.tensor_copy(RW1[V_LD:V_LD + Q, :].rearrange("p (b n) -> p b n", b=2),
                            LDT[V_LD:V_LD + Q, :].unsqueeze(2).to_broadcast([Q, 2, NS])), ldt_ready)
            wait_filled(dve, ("vec",))
            evac(dve, v.tensor_copy(V[:, :], bank(("vec",))[:, 0:116]), ("vec",), own=True)
            dve.sem_inc(v_done, 1)
            wait_filled(dve, ("bgu",))
            evac(dve, v.tensor_copy(BGU[:, :], bank(("bgu",))), ("bgu",))
            for w, u in enumerate((("cre",), ("cim",))):
                wait_filled(dve, u)
                o = bank(u).rearrange("p (q b c) -> p q b c", q=Q, b=2)
                d(v.tensor_scalar(CC[0:NS, w, :, :], o[0:NS, :, 0, :], -1.0 if w else 1.0, None, mul))
                evac(dve, v.tensor_scalar(CC[NS:P, w, :, :], o[NS:P, :, 1, :], -1.0 if w else 1.0, None, mul),
                     u, own=True)

            def rstd(n, l, c0):
                dve.wait_ge(ssq_done[n], l + 1)
                d(v.reciprocal(sm[:, c0 + 16:c0 + 17], sm[:, c0 + 8:c0 + 9]), rstd_done[n])

            def scaled(u, dst, g0, n=4):
                wait_filled(dve, u)
                evac(dve, v.tensor_tensor(dst, bank(u).rearrange("p (k s) -> p k s", k=n),
                                          V[:, g0:g0 + n].unsqueeze(2).to_broadcast([P, n, HALF // n]), mul), u)

            def norm_tiles(kind, n, gain):
                for l in range(L + 1):
                    if l < L:
                        rstd(n, l, l)
                    if l:
                        for h in range(2):
                            scaled((kind, l - 1, h), XT[:, 4 * h:4 * h + 4, (l - 1) * P:l * P], gain + 4 * h)

            norm_tiles("xt", 0, V_MIX)
            dve.wait_ge(xn_done[0], L)
            d(v.memset(XRg[:, 0:4], 0.0), xr_zero)

            dt, mg, sn, cs = sm[:, 24:40], sm[:, 40:56], sm[:, 56:72], sm[:, 72:88]
            mag8, uc, us = sm[:, 128:144], sm[:, 144:160], sm[:, 160:176]
            LR, LI = V[:, V_LR:V_LR + Q], V[:, V_LI:V_LI + Q]
            S = [SCR[:, n * Q:(n + 1) * Q] for n in range(14)]
            dve.wait_ge(dt_done, 1)
            tt(mg, dt, LR, mul, s=ang_done)
            ts(S[1], V[:, V_LI:V_LI + Q], 1.0, None, mul)
            tt(S[0], dt, LI, mul)
            ts(S[1], S[0], 1.0 / (2 * math.pi), None, mul)
            ts(S[1], S[1], 1.5 * 2 ** 23, None, add)
            ts(S[1], S[1], 1.5 * 2 ** 23, None, sub)
            C1 = 6.28125
            C2 = float(np.float32(2 * math.pi - C1) // 2.0 ** -22 * 2.0 ** -22)
            for c in (C1, C2, 2 * math.pi - C1 - C2):
                stt(S[0], S[1], -c, S[0], mul, add)
            BOUND = 3.1415925
            ts(sn, S[0], BOUND, -BOUND, ALU.min, ALU.max)
            ts(S[2], S[0], math.pi / 2, None, add)
            ts(S[3], S[2], math.pi, -2 * math.pi, ALU.is_gt, mul)
            tt(S[2], S[2], S[3], add)
            ts(cs, S[2], BOUND, -BOUND, ALU.min, ALU.max, s=ang_done)
            lam = V[:, V_LAM:V_LAM + CT]
            z = sm[:, 88:92]
            ts(z, lam, -1.0, None, mul)
            tt(z, z, lam, ALU.min, s=ang_done)
            dve.wait_ge(trig_done, 1)
            are, aim = PW[:, 0, :, 1], PW[:, 1, :, 1]
            tt(are, mg, cs, mul)
            tt(aim, mg, sn, mul)
            ts(S[4], are, 1.0, None, sub)
            tt(S[5], LR, LR, mul)
            tt(S[6], LI, LI, mul)
            tt(S[5], S[5], S[6], add)
            d(v.reciprocal(S[5], S[5]))
            tt(S[6], S[4], LR, mul)
            tt(S[7], aim, LI, mul)
            tt(S[6], S[6], S[7], add)
            tt(S[6], S[6], S[5], mul)
            tt(S[7], aim, LR, mul)
            tt(S[8], S[4], LI, mul)
            tt(S[7], S[7], S[8], sub)
            tt(S[7], S[7], S[5], mul)

            def wide(x):
                return x.unsqueeze(2).to_broadcast([P, Q, SC])

            B0, B1 = BRW[:, 0, :, :], BRW[:, 1, :, :]
            dve.wait_ge(par_in, 16 * 10)
            tt(BB[:, 0], wide(S[6]), B0, mul)
            tt(TMB, wide(S[7]), B1, mul)
            tt(BB[:, 0], BB[:, 0], TMB, sub)
            tt(BB[:, 1], wide(S[6]), B1, mul)
            tt(TMB, wide(S[7]), B0, mul)
            tt(BB[:, 1], BB[:, 1], TMB, add)
            d(v.memset(PW[:, 0, :, 0], 1.0))
            d(v.memset(PW[:, 1, :, 0], 0.0))

            def cmul(ore, oim, xr_, xi, yr, yi, t1, t2, s=dve_step):
                tt(t1, xr_, yr, mul)
                tt(t2, xi, yi, mul)
                tt(ore, t1, t2, sub)
                tt(t1, xr_, yi, mul)
                tt(t2, xi, yr, mul)
                tt(oim, t1, t2, add, s=s)

            for n in (1, 2, 4):
                x = [PW[:, r, :, 1:n + 1] for r in range(2)]
                y = [PW[:, r, :, n:n + 1].to_broadcast([P, Q, n]) for r in range(2)]
                t1 = SCR[:, 224:224 + Q * n].rearrange("p (q n) -> p q n", q=Q)
                t2 = SCR[:, 288:288 + Q * n].rearrange("p (q n) -> p q n", q=Q)
                cmul(PW[:, 0, :, n + 1:2 * n + 1], PW[:, 1, :, n + 1:2 * n + 1], x[0], x[1], y[0], y[1], t1, t2)
            for j in range(L):
                for r in range(2):
                    d(v.tensor_copy(QV[:, r, :, j], PW[:, r, :, L - 1 - j]))
            tt(S[9], mg, mg, mul)
            tt(S[9], S[9], S[9], mul)
            tt(mag8, S[9], S[9], mul)
            cmul(S[10], S[11], cs, sn, cs, sn, S[12], S[13])
            cmul(S[8], S[9], S[10], S[11], S[10], S[11], S[12], S[13])
            cmul(uc, us, S[8], S[9], S[8], S[9], S[12], S[13], s=bb_done)

            w, w2, ac = S[0][:, 0:CT], S[1][:, 0:CT], S[2][:, 0:CT]
            ts(w, z, 2.0, None, add)
            d(v.reciprocal(w, w))
            tt(w, w, z, mul)
            tt(w2, w, w, mul)
            ts(ac, w2, 1.0 / 19, 1.0 / 17, mul, add)
            for n in (15, 13, 11, 9, 7, 5, 3, 1):
                tt(ac, ac, w2, mul)
                ts(ac, ac, 1.0 / n, None, add)
            tt(ac, ac, w, mul)
            ts(w, lam, -1.0, 0.0, mul, ALU.max)
            stt(w, ac, 2.0, w, mul, add)
            ts(sm[:, 92:96], V[:, V_BA:V_BA + CT], 0.5, None, mul)
            ts(sm[:, 96:100], V[:, V_BX:V_BX + CT], 0.5, None, mul)
            ts(sm[:, 100:104], w, RG_C / 4, None, mul, s=rgc_done)

            def conv(ct):
                for h in range(2):
                    s = emptied[number[("xr", ct, h)] % 8]
                    dve.wait_ge(s, number[("xr", ct, h)] // 8 + 1)
                wk = [V[:, V_CW + k * CT + ct:V_CW + k * CT + ct + 1] for k in range(CW)]
                ts(XC, XRg[:, 0:T], wk[0], V[:, V_CB + ct:V_CB + ct + 1], mul, add)
                for k in range(1, CW):
                    stt(XC, XRg[:, k:k + T], wk[k], XC, mul, add, s=xc_done if k == CW - 1 else dve_step)

            conv(0)
            dve.wait_ge(db_done, 1)
            for b in range(2):
                u = ("ktap", b)
                wait_filled(dve, u)
                evac(dve, v.tensor_tensor(KTS.rearrange("p (q b c) -> p b q c", q=Q, b=2)[:, b],
                                          bank(u)[:, 0:Q * SC].rearrange("p (q c) -> p q c", q=Q),
                                          DB.rearrange("p (q b c) -> p b q c", q=Q, b=2)[:, b], add), u, own=True)
            dve.sem_inc(kts_done, 1)
            for ct in range(CT):
                dve.wait_ge(rg_tp, ct + 1)
                ts(QQ, TH, 1.0, None, add, s=rg_q)
                d(v.reciprocal(QQ, QQ))
                stt(TI, TI, 1.0, XC, add, mul)
                ts(XC, QQ, 2.0, -1.0, mul, add)
                dve.wait_ge(rg_sq, ct + 1)
                tt(QQ, QQ, TH, mul)
                d(v.memset(QQ[:, 0:1], 0.5))
                tt(TI, TI, QQ, mul)
                d(v.tensor_tensor_scan(QQ, XC, TI, 0.0, mul, add))
                if ct == 2:
                    dve.wait_ge(mm_in, 16 * L)
                for h in range(2):
                    dve.wait_ge(emptied[number[("g", ct, h)] % 8], number[("g", ct, h)] // 8 + 1)
                tt(YT[:, ct, :].rearrange("p (l k) -> p k l", l=L), QQ.rearrange("p (k l) -> p k l", l=L),
                   GT[:, ct % 2, :].rearrange("p (k l) -> p k l", l=L), mul, s=rg_done)
                if ct + 1 < CT:
                    conv(ct + 1)

            dve.wait_ge(rot_done, 1)
            for n in range(4):
                sl = slice(4 * n, 4 * n + 4)
                cr = RT[:, 0, sl, :].rearrange("p q k -> p (q k)")
                ci = RT[:, 1, sl, :].rearrange("p q k -> p (q k)")
                wait_filled(dve, ("s", 0, n))
                wait_filled(dve, ("s", 1, n))
                sre, sim = bank(("s", 0, n)), bank(("s", 1, n))
                ore, oim = (SR[:, r, sl, :].rearrange("p q k -> p (q k)") for r in range(2))
                tt(TA, cr, sre, mul)
                tt(TB, ci, sim, mul)
                tt(ore, TA, TB, add)
                d(v.tensor_tensor(TA, cr, sim, mul))
                evac(dve, v.tensor_tensor(TB, ci, sre, mul), ("s", 0, n), own=True)
                evac(dve, v.tensor_tensor(oim, TA, TB, sub), ("s", 1, n), own=True)
                for r in range(2):
                    for q in range(4 * n, 4 * n + 4):
                        d(v.tensor_tensor_scan(SR[:, r, q, :], mag8[:, q:q + 1].to_broadcast([P, P]),
                                               SR[:, r, q, :], 0.0, mul, add))
            d(v.memset(HP[:, :, :, 0], 0.0))
            n = P - 1
            cr, ci = RT[:, 0, :, 0:n], RT[:, 1, :, 0:n]
            hr, hi = SR[:, 0, :, 0:n], SR[:, 1, :, 0:n]
            cmul(HP[:, 0, :, 1:], HP[:, 1, :, 1:], cr, ci, hr, hi, T1[:, :, 0:n], T2[:, :, 0:n], s=hp_done)
            for n in range(2 * CT):
                cb, h = divmod(n, 2)
                u = ("glu", cb, h)
                dve.wait_ge(emptied[number[u] % 8], number[u] // 8 + 1)
                y = YT[:, CT + cb, h * HALF:(h + 1) * HALF]
                tt(y, y, SG[:, n % 2, :], mul, s=glu_done)
            dve.wait_ge(x_again, 16)
            for c in range(2):
                for l in range(L):
                    u = ("wo1", c, l)
                    cc = slice(c * HALF, (c + 1) * HALF)
                    wait_filled(dve, u)
                    evac(dve, v.tensor_tensor(H[:, l, cc], bank(u), XR0[:, l, cc], add), u, own=True)
                    dve.sem_inc(h1_done, 1)
                if c == 0:
                    for m in range(MT):
                        rstd(1, m, 104 + m)
            for m in range(MT):
                for h in range(2):
                    scaled(("mt", m, h), MEMT[:, 4 * h:4 * h + 4, m * P:(m + 1) * P], V_MEM + 4 * h)
            norm_tiles("xt2", 2, V_XA)

            def maxima(n):
                u = ("sc",) + att[n]
                c = 24 + 2 * (n % 2)
                wait_filled(dve, u)
                d(v.tensor_reduce(MXT[:, 0:2], bank(u).rearrange("p (h m) -> p h m", h=2), AX.X, ALU.max))
                ts(sm[:, c:c + 2], MXT[:, 0:2], -HD ** -0.5, None, mul, s=mx_done)

            def normalise(n):
                b = n % 2
                dve.wait_ge(exp_done, 2 * n + 2)
                d(v.reciprocal(sm[:, 32:34], sm[:, 28 + 2 * b:30 + 2 * b]))
                tt(PP[:, b, :, :], PP[:, b, :, :], sm[:, 32:34].unsqueeze(2).to_broadcast([P, 2, ML]), mul, s=pn_done)

            def keep(n):
                l, hp = att[n]
                u = ("pt", l, hp)
                wait_filled(dve, u)
                evac(dve, v.tensor_copy(PT[:, 2 * hp:2 * hp + 2, :, l * P:(l + 1) * P],
                                        bank(u).rearrange("p (h m t) -> p h m t", h=2, m=MT)), u)

            for n in range(len(att) + LEAD):
                if n < len(att):
                    maxima(n)
                if 0 < n <= len(att):
                    normalise(n - 1)
                if n >= LEAD:
                    keep(n - LEAD)
            for c in range(2):
                for l in range(L):
                    u = ("wo2", c, l)
                    cc = slice(c * HALF, (c + 1) * HALF)
                    wait_filled(dve, u)
                    evac(dve, v.tensor_tensor(H[:, l, cc], bank(u), H[:, l, cc], add), u, own=True)
                    dve.sem_inc(h2_done, 1)
            norm_tiles("xt3", 3, V_FFN)

            wait_filled(dve, ("rt",))
            dve.wait_ge(rt_in, 32)
            evac(dve, v.tensor_tensor(LG, bank(("rt",))[:, 0:L * E].rearrange("p (l e) -> p l e", l=L),
                                      RB.unsqueeze(1).to_broadcast([P, L, E]), add), ("rt",), own=True)
            for l in range(L):
                d(v.max(TV[:, l, :], LG[:, l, :]))
                d(v.max_index(TIu[:, l, :], TV[:, l, :], LG[:, l, :]))
            d(v.tensor_copy(TIf, TIu))
            tt(GW, TV[:, :, 0:TOPK], TV[:, :, 0:1].to_broadcast([P, L, TOPK]), sub, s=gexp_in)
            dve.wait_ge(iota_done, 3)
            OH4 = OH.rearrange("p j (l e) -> p j l e", l=L)
            for j in range(TOPK):
                tt(OH4[:, j], TIf[:, :, j:j + 1].to_broadcast([P, L, E]), IO.unsqueeze(1).to_broadcast([P, L, E]),
                   ALU.is_equal)
            tt(MS, OH4[:, 0], OH4[:, 1], add)
            tt(MS, MS, OH4[:, 2], add)
            tt(MS, MS, OH4[:, 3], add)
            d(v.memset(CU[:, 0, :], 0.0))
            for l in range(L):
                tt(CU[:, l + 1, :], CU[:, l, :], MS[:, l, :], add, s=ms_done if l == L - 1 else dve_step)
            dve.wait_ge(gexp_done, 1)
            d(v.tensor_reduce(MXT[:, 0:L], GW, AX.X, add))
            d(v.reciprocal(MXT[:, 0:L], MXT[:, 0:L]))
            tt(GW, GW, MXT[:, 0:L].unsqueeze(2).to_broadcast([P, L, TOPK]), mul)
            for j in range(TOPK):
                t = GF if j == 0 else MTM
                tt(t, OH4[:, j], GW[:, :, j:j + 1].to_broadcast([P, L, E]), mul)
                if j:
                    tt(GF, GF, MTM, add, s=gf_done if j == TOPK - 1 else dve_step)
            wait_filled(dve, ("rank",))
            wait_filled(dve, ("cnt",))
            evac(dve, v.tensor_copy(CNT, bank(("cnt",))[:, 0:E]), ("cnt",), own=True)
            ts(NTI, CNT, float(W), 1.0, ALU.is_gt, add)
            for n in range(2, T // W):
                ts(IT1, CNT, float(n * W), None, ALU.is_gt)
                tt(NTI, NTI, IT1, add)
            d(v.tensor_tensor_scan(PEN, ones[:, 0:E], NTI, 0.0, mul, add))
            tt(PST, PEN, NTI, sub)
            ts(IT1, PST, float(W), None, mul)
            evac(dve, v.tensor_tensor(SL.rearrange("p (l e) -> p l e", l=L),
                                      bank(("rank",))[:, 0:L * E].rearrange("p (l e) -> p l e", l=L),
                                      IT1.unsqueeze(1).to_broadcast([P, L, E]), add), ("rank",), own=True)
            d(v.tensor_tensor_scan(CX, ones[:, 0:E], CNT, 0.0, mul, add))
            tt(CX, CX, CNT, sub)
            tt(IT2, CX, IT1, sub)
            tt(SLY.rearrange("p (l e) -> p l e", l=L), SL.rearrange("p (l e) -> p l e", l=L),
               IT2.unsqueeze(1).to_broadcast([P, L, E]), add)
            tt(OHS, OH, SLY.unsqueeze(1).to_broadcast([P, TOPK, L * E]), mul)
            d(v.tensor_reduce(POSf, OHS.rearrange("p j (l e) -> p (j l) e", l=L), AX.X, add))
            d(v.tensor_copy(POSY, POSf))
            tt(OHS, OH, SL.unsqueeze(1).to_broadcast([P, TOPK, L * E]), mul)
            d(v.tensor_reduce(POSf, OHS.rearrange("p j (l e) -> p (j l) e", l=L), AX.X, add))
            d(v.tensor_copy(POS, POSf), pos_done)
            tt(CNT, CNT, IT1, add)
            ts(IT2, PEN, IOP, None, ALU.is_le)
            ts(IT3, PST, IOP, None, ALU.is_le)
            d(v.tensor_reduce(ITE[:, 0:1], IT2, AX.X, add))
            ts(ITE[:, 0:1], ITE[:, 0:1], float(E - 1), None, ALU.min)
            tt(IT3, IT3, IT2, sub)
            d(v.tensor_reduce(MXT[:, 0:1], IT3, AX.X, add))
            tt(IT2, IT3, CNT, mul)
            d(v.tensor_reduce(MXT[:, 1:2], IT2, AX.X, add))
            tt(IT4, CX, IT1, sub)
            tt(IT4, IT4, IT3, mul)
            d(v.tensor_reduce(MXT[:, 3:4], IT4, AX.X, add))
            ts(MXT[:, 4:5], IOP, float(W), None, mul)
            tt(MXT[:, 3:4], MXT[:, 3:4], MXT[:, 4:5], add)
            tt(ITE[:, 2:3], MXT[:, 3:4], MXT[:, 0:1], mul)
            ts(MXT[:, 2:3], IOP, -float(W), None, mul)
            tt(MXT[:, 1:2], MXT[:, 1:2], MXT[:, 2:3], add)
            ts(MXT[:, 1:2], MXT[:, 1:2], 1.0, float(W), ALU.max, ALU.min)
            tt(ITE[:, 1:2], MXT[:, 1:2], MXT[:, 0:1], mul, s=ite_done)
            wait_filled(dve, ("itm",))
            evac(dve, v.tensor_copy(ITM, bank(("itm",))[0:1, 0:3 * P]), ("itm",), own=True)
            dve.sem_inc(itm_done, 1)
            for l in range(L):
                for c in range(2):
                    u = ("bd", l, c)
                    cc = slice(c * HALF, (c + 1) * HALF)
                    wait_filled(dve, u)
                    evac(dve, v.tensor_tensor(H[:, l, cc], bank(u), H[:, l, cc], add), u, own=True)
            dve.wait_ge(tb_in, 16)
            d(v.tensor_copy(TBF[0:NROW, :], TBI[0:NROW, :]), tbf_done)
            wait_filled(dve, ("idx",))
            evac(dve, v.tensor_copy(IDX[:, 0:NROW], bank(("idx",))[:, 0:NROW]), ("idx",), own=True)
            dve.sem_inc(idx_done, 1)

            dve.sem_inc(gb_free, 2)
            with dve.Fori(0, ITEMS) as i:
                n_i = item_tokens(dve, i)
                e_i = item_expert(dve, i)

                def item(n):
                    v.tensor_copy(BGC, BGU[:, bass.ds(e_i * (2 * FT), 2 * FT)]).then_inc(bgc_done, 1)
                    dve.wait_ge(bgc_done, i + 1)

                    def finish(f):
                        b = f % 2
                        dve.wait_ge(si_done, 8 * i + f + 1)
                        v.tensor_tensor(GA[:, b, 0:n], GA[:, b, 0:n], SI[:, b, 0:n], mul).then_inc(ffn_step, 1)
                        dve.wait_ge(ffn_step, 16 * i + 2 * f + (3 if f < FT - 1 else 2))
                        v.tensor_tensor(HT[:, f, 0:n], GA[:, b, 0:n], UP[:, b, 0:n], mul).then_inc(ht_done, 1)

                    for f in range(FT):
                        b = f % 2
                        if f >= 2:
                            dve.wait_ge(ht_done, 8 * i + f - 1)
                        dve.wait_ge(gb_filled, 8 * i + f + 9)
                        v.tensor_scalar(GA[:, b, 0:n], PS[:, b, 0:n], BGC[:, f:f + 1], LIMIT, add, ALU.min) \
                            .then_inc(ga_done, 1)
                        v.tensor_scalar(UP[:, b, 0:n], PS[:, b, W:W + n], BGC[:, FT + f:FT + f + 1], LIMIT,
                                        add, ALU.min).then_inc(gb_free, 1)
                        dve.wait_ge(gb_free, 8 * i + f + 3)
                        v.tensor_scalar(UP[:, b, 0:n], UP[:, b, 0:n], -LIMIT, 1.0, ALU.max, add).then_inc(ffn_step, 1)
                        if f:
                            finish(f - 1)
                    finish(FT - 1)

                by_width(dve, n_i, item)

            dve.wait_ge(fg_in, 16)

            def last_norm(l):
                dve.wait_ge(ssq_done[4], l + 1)
                d(v.reciprocal(sm[:, l + 16:l + 17], sm[:, l + 8:l + 9]))
                stt(H[:, l, :], H[:, l, :], sm[:, l + 16:l + 17], FG, mul, mul, s=out_ready)

            for l in range(L):
                dve.wait_ge(cb_in[l % 2], 16 * TOPK * (l // 2 + 1))
                for j in range(TOPK):
                    stt(H[:, l, :], CB[:, l % 2, j, :], GW[:, l, j:j + 1], H[:, l, :], mul, add,
                        s=comb_done if j == TOPK - 1 else dve_step)
                if l:
                    last_norm(l - 1)
            last_norm(L - 1)

        @block.gpsimd
        def _(pool):
            g = nc.gpsimd
            mul, add, sub = ALU.mult, ALU.add, ALU.subtract

            def d(ins, s=pool_step):
                link(pool, ins, s)

            def tt(o, x, y, op, s=pool_step):
                d(g.tensor_tensor(o, x, y, op), s)

            d(g.memset(ident[:], 0.0))
            d(g.affine_select(out=ident[:], in_=ident[:], compare_op=ALU.not_equal, fill=1.0, base=0,
                              pattern=[[-1, P]], channel_multiplier=1), consts)
            d(g.memset(ones[:], 1.0), consts)
            for t in (BA, BX, BG):
                d(g.memset(t[:], 0.0), zeroed)
            d(g.iota(IOI, pattern=[[1, E]], base=0, channel_multiplier=0))
            d(g.tensor_copy(IO, IOI), iota_done)
            d(g.iota(IOI[:, 0:1], pattern=[[1, 1]], base=0, channel_multiplier=1))
            d(g.tensor_copy(IOP, IOI[:, 0:1]), iota_done)
            d(g.iota(TOKI, pattern=[[1, L]], base=0, channel_multiplier=L), iota_done)
            pool.wait_ge(d_in, 16)
            d(g.affine_select(out=DB.rearrange("p (g c) -> p g c", g=G), in_=DB.rearrange("p (g c) -> p g c", g=G),
                              compare_op=ALU.is_equal, fill=0.0, base=-(L - 1) * SC,
                              pattern=[[0, G], [-1, SC]], channel_multiplier=1), db_done)

            pool.wait_ge(bb_done, 1)

            def b4(x):
                return x.unsqueeze(2).to_broadcast([P, Q, L, SC])

            def p4(x):
                return x.unsqueeze(3).to_broadcast([P, Q, L, SC])

            TG1 = wa(8192, Q, L, SC)
            TG2 = wa(8192 + 2048, Q, L, SC)
            for r in range(2):
                tt(TG1, p4(QV[:, 0]), b4(BB[:, r]), mul)
                tt(TG2, p4(QV[:, 1]), b4(BB[:, 1 - r]), mul)
                tt(GM[:, r], TG1, TG2, add if r else sub, s=g_done if r else pool_step)
            pool.wait_ge(kts_done, 1)
            d(g.memset(RT[:, 0, :, 0:1], 1.0))
            d(g.memset(RT[:, 1, :, 0:1], 0.0))
            uc, us = sm[:, 144:160], sm[:, 160:176]
            n = 1
            while n < P:
                t1, t2 = TG1.rearrange("p a b c -> p (a b c)"), TG2.rearrange("p a b c -> p (a b c)")
                t1 = t1[:, 0:Q * n].rearrange("p (q n) -> p q n", q=Q)
                t2 = t2[:, 0:Q * n].rearrange("p (q n) -> p q n", q=Q)
                c, s_ = (x.unsqueeze(2).to_broadcast([P, Q, n]) for x in (uc, us))
                tt(t1, RT[:, 0, :, 0:n], c, mul)
                tt(t2, RT[:, 1, :, 0:n], s_, mul)
                tt(RT[:, 0, :, n:2 * n], t1, t2, sub)
                tt(t1, RT[:, 0, :, 0:n], s_, mul)
                tt(t2, RT[:, 1, :, 0:n], c, mul)
                tt(RT[:, 1, :, n:2 * n], t1, t2, add)
                n *= 2
                if n < P:
                    a1, a2, a3 = (TG1.rearrange("p a b c -> p (a b c)")[:, Q * k:Q * k + Q] for k in range(3))
                    tt(a1, uc, uc, mul)
                    tt(a2, us, us, mul)
                    tt(a3, uc, us, mul)
                    tt(uc, a1, a2, sub)
                    tt(us, a3, a3, add)
            pool.sem_inc(rot_done, 1)
            d(g.memset(MM, 0.0))
            pool.dma_start(slot_tok.rearrange("(r p) o -> r (p o)", p=P),
                           MM[0:NROW, 0, 0:P].bitcast(I32)).then_inc(zero_out, 16)
            pool.wait_ge(zero_out, 16)
            for l in range(L):
                pool.dma_start(MM[0:(l + 1) * SC, l, :], KTS[(L - 1 - l) * SC:P, :]).then_inc(mm_in, 16)
            pool.wait_ge(rg_done, CT)
            TF1 = Hf[:, 5120:6144].rearrange("p (q l c) -> p q l c", q=Q // 2, l=L)
            TF2 = Hf[:, 6144:7168].rearrange("p (q l c) -> p q l c", q=Q // 2, l=L)
            for hq in range(2):
                qs = slice(hq * Q // 2, (hq + 1) * Q // 2)
                sh = [P, Q // 2, L, SC]
                c0, c1 = (CC[:, r, qs].unsqueeze(2).to_broadcast(sh) for r in range(2))
                w0, w1 = (PW[:, r, qs, 1:9].unsqueeze(3).to_broadcast(sh) for r in range(2))
                tt(TF1, c0, w0, mul)
                tt(TF2, c1, w1, mul)
                tt(FM[:, 0, qs], TF1, TF2, add)
                tt(TF1, c1, w0, mul)
                tt(TF2, c0, w1, mul)
                tt(FM[:, 1, qs], TF1, TF2, sub, s=f_done if hq else pool_step)
            pool.wait_ge(h2_done, 2 * L)
            d(g.affine_select(out=TRI, in_=ones[:], compare_op=ALU.is_gt, fill=0.0, base=0,
                              pattern=[[1, P]], channel_multiplier=-1), tri_done)
            pool.wait_ge(pos_done, 1)
            for j in range(TOPK):
                for l in range(L):
                    g.indirect_dma_start(out=slot_tok[:, :],
                                         out_offset=bass.IndirectOffsetOnAxis(ap=POS[:, j * L + l:j * L + l + 1], axis=0),
                                         in_=TOKI[:, l:l + 1], in_offset=None).then_inc(scat, 16)
            pool.wait_ge(scat, 16 * TOPK * L)
            pool.wait_ge(xn_out, 16 * L)

            def gather():
                for t in range(2):
                    g.indirect_dma_start(out=XG[:, t, :], out_offset=None, in_=xn_rows[:, :],
                                         in_offset=bass.IndirectOffsetOnAxis(ap=IDC[:, t:t + 1], axis=0)) \
                        .then_inc(xg_in, 16)

            pool.wait_ge(idx_done, 1)
            pool.wait_ge(itm_done, 1)
            g.memset(YS[:, 1, :], 0.0).then_inc(y_zero, 1)
            pool.wait_ge(y_zero, 1)
            pool.sem_inc(ys_free, 1)
            g.tensor_copy(IDC, IDX[:, 0:2]).then_inc(idc_done, 1)
            pool.wait_ge(idc_done, 1)
            gather()
            with pool.Fori(0, ITEMS) as i:
                n_i = item_tokens(pool, i)

                def row(t):
                    return pool.value_load(ITM[0:1, bass.ds(i + 2 * P, 1)], min_val=0, max_val=T * TOPK) + t * P

                def fetch_and_store(store):
                    pool.wait_ge(xg_in, 32 * i + 32)
                    g.tensor_copy(IDC, IDX[:, bass.ds(2 * i + 2, 2)]).then_inc(idc_done, 1)
                    pool.wait_ge(idc_done, i + 2)
                    pool.wait_ge(xe_filled, 4 * i + 4)
                    pool.sem_inc(gather_go, 1)
                    gather()
                    pool.wait_ge(y_done, i + 2)
                    store()
                    pool.wait_ge(y_out, 32 * i + 32)
                    pool.sem_inc(ys_free, 1)

                def store_one():
                    pool.dma_start(y_rows[bass.ds(row(0), P), :], YS[:, 0, :]).then_inc(y_out, 32)

                def store_two():
                    pool.dma_start(y_rows[bass.ds(row(0), P), :], YS[:, 0, :]).then_inc(y_out, 16)
                    pool.dma_start(y_rows[bass.ds(row(1), P), :], YS[:, 1, :]).then_inc(y_out, 16)

                with pool.If(n_i > 0):
                    with pool.If(n_i > P):
                        fetch_and_store(store_two)
                    with pool.Else():
                        fetch_and_store(store_one)
            for l in range(L):
                if l >= 2:
                    pool.wait_ge(comb_done, l - 1)
                for j in range(TOPK):
                    g.indirect_dma_start(out=CB[:, l % 2, j, :], out_offset=None, in_=y_rows[0:T * TOPK, :],
                                         in_offset=bass.IndirectOffsetOnAxis(ap=POSY[:, j * L + l:j * L + l + 1], axis=0)) \
                        .then_inc(cb_in[l % 2], 16)


def kernel(**inputs):
    import numpy as _np
    import concourse.bacc as _bacc
    from concourse import mybir as _mybir
    from concourse.bass_utils import run_bass_kernel_spmd as _run

    nc = _bacc.Bacc("TRN2", target_bir_lowering=False, num_devices=1)
    arrays, args = {}, {}
    for name in NAMES:
        a = _np.ascontiguousarray(inputs[name])
        arrays[f"in_{name}"] = a
        args[name] = nc.dram_tensor(f"in_{name}", a.shape, _mybir.dt.from_np(a.dtype), kind="ExternalInput").ap()
    out = nc.dram_tensor("out", arrays["in_x"].shape, _mybir.dt.float32, kind="ExternalOutput").ap()
    build(nc, args, out)
    return _run(nc, [arrays], core_ids=[0]).results[0]["out"]
```

```python
import math

import numpy as np
import concourse.bass as bass
import concourse.mybir as mybir
from contextlib import ExitStack, contextmanager

F32 = mybir.dt.float32
F32R = mybir.dt.float32r
I32 = mybir.dt.int32
U32 = mybir.dt.uint32
ALU = mybir.AluOpType
ACT = mybir.ActivationFunctionType
AX = mybir.AxisListType

P = 128
NAMES = ["x", "mem", "norm_mix_g", "w_in", "conv_w", "conv_b", "rg_wa", "rg_ba", "rg_wx", "rg_bx",
         "rg_lambda", "s5_lambda_re", "s5_lambda_im", "s5_b_re", "s5_b_im", "s5_c_re", "s5_c_im",
         "s5_d", "s5_log_dt", "s5_glu_w", "s5_glu_b", "w_out", "norm_xa_g", "mem_norm_g", "xa_wq",
         "xa_wkv", "xa_wo", "norm_ffn_g", "router_w", "router_b", "exp_w_gu", "exp_b_gu",
         "exp_w_down", "exp_b_down", "final_norm_g"]


def build(nc, A, out):
    D = A["w_in"].shape[0]
    T = A["x"].shape[1]
    L = T // P
    K = D // P
    CW = A["conv_w"].shape[0]
    CT = A["conv_b"].shape[0] // P
    G, NS = A["s5_lambda_re"].shape
    SC = A["s5_b_re"].shape[2]
    Q = G // 2
    MT = A["mem"].shape[1] // P
    ML = A["mem"].shape[1]
    NH = 4
    HD = D // NH
    E = A["router_w"].shape[1]
    TOPK = 4
    W = 256
    FT = D // P
    ITEMS = (T * TOPK + E * W) // W
    GROUP = 16
    POOL_TILES = 5
    EPS = 1e-6
    HALF = 512
    LIMIT, ALPHA = 7.0, 1.702
    RG_C = 8.0

    ctx = ExitStack()
    with ctx:
        def sb(name, shape, dt=F32):
            return ctx.enter_context(nc.sbuf_tensor(name, shape, dt))

        def sem(name):
            return ctx.enter_context(nc.semaphore(name))

        WA = sb("WA", [P, 16384])
        H = sb("H", [P, L, D])
        ident = sb("ident", [P, P])
        ones = sb("ones", [P, P])
        V = sb("V", [P, 116])
        BGU = sb("BGU", [P, 2 * FT * E])
        PW = sb("PW", [P, 2, Q, 9])
        sm = sb("sm", [P, 256])
        IOI_ = sb("iota", [P, 32], I32)
        PS = ctx.enter_context(nc.psum_tensor("PS", [P, 8, HALF], F32))

        with ExitStack() as first:
            def sb1(name, shape):
                return first.enter_context(nc.sbuf_tensor(name, shape, F32))

            WB = sb1("WB", [P, 8192])
            XT = sb1("XT", [P, K, T])
            YT = sb1("YT", [P, K, T])
            MW = sb1("MW", [P, 3 * CT * P + 4 * Q * SC])
        DNW = sb("DNW", [P, 2, 2, D])
        DNH = sb("DNH", [P, 4, D], F32R)
        XG = sb("XG", [P, 2, D])
        XE = sb("XE", [P, K, W])
        HTH = sb("HTH", [P, FT, W], F32R)
        YS = sb("YS", [P, 2, D])
        DNL = sb("DNL", [P, 4, D], F32R)
        sb("YT_upper", [P, K * T // 2])
        HTL = sb("HTL", [P, FT, W], F32R)
        BA, BX, BG = (MW[:, n * CT * P:(n + 1) * CT * P].rearrange("p (c n) -> p c n", c=CT)
                      for n in range(3))
        CC, BB = (MW[:, (3 * CT * P + 2 * n * Q * SC):(3 * CT * P + 2 * (n + 1) * Q * SC)]
                  .rearrange("p (r q c) -> p r q c", r=2, q=Q)
                  for n in range(2))

        def wa(off, *dims):
            n = int(np.prod(dims))
            v = WA[:, off:off + n]
            if len(dims) == 1:
                return v
            names = "abcd"[:len(dims)]
            return v.rearrange("p (" + " ".join(names) + ") -> p " + " ".join(names),
                               **{a: d for a, d in zip(names, dims)})

        GM = wa(0, 2, Q, L, SC)
        SR = wa(0, 2, Q, P)
        EM = wa(4096, 2, Q, P)
        MM = wa(8192, L, G * SC)
        RT = wa(12288, 2, Q, P)
        T1 = wa(4096, Q, P)
        T2 = wa(4096 + Q * P, Q, P)
        RW1 = wa(12288, P)
        BGR = wa(12288 + 128, 4, P)
        CRW = wa(12288 + 640, 2, 4, 2, NS)
        BRW = wa(12288 + 1664, 2, Q, SC)
        TMB = wa(12288 + 2692, Q, SC)
        LDT = wa(12288 + 2690, 2)
        SCR = wa(12288 + 2948, 352)
        QV = wa(12288 + 3300, 2, Q, L)
        DB = wa(12288 + 3556, HALF)
        XR0 = wa(0, L, D)
        KT = wa(8192, K, ML)
        VV = wa(10240, MT, D)
        MEM = wa(12288, MT, D)
        MEMT = wa(14336, K, ML)
        PP = wa(0, 2, 2, ML)
        PT = XT[:, :, :].rearrange("p k t -> p (k t)").rearrange("p (h m t) -> p h m t", h=NH, m=MT)
        Hf = H[:, :, :].rearrange("p l d -> p (l d)")
        XRg = Hf[:, 0:T + 4]
        GT = Hf[:, 1028:1028 + 2 * T].rearrange("p (b t) -> p b t", b=2)
        XC, TH, TI, QQ = (Hf[:, 3076 + n * T:3076 + (n + 1) * T] for n in range(4))
        HP = Hf[:, 0:4096].rearrange("p (r q k) -> p r q k", r=2, q=Q)
        YTK = Hf[:, 4096:8192].rearrange("p (l c) -> p l c", l=L)
        XTf = XT[:, :, :].rearrange("p k t -> p (k t)")
        SG = XTf[:, 0:2 * HALF].rearrange("p (b n) -> p b n", b=2)
        SQ = XTf[:, 0:2 * D].rearrange("p (b n) -> p b n", b=2)
        UT = XTf[:, 0:4096].rearrange("p (g k) -> p g k", g=G)
        FM = XTf[:, 4096:8192].rearrange("p (r q l c) -> p r q l c", r=2, q=Q, l=L)
        YTf = YT[:, :, :].rearrange("p k t -> p (k t)")
        TA, TB = YTf[:, 4096:4096 + HALF], YTf[:, 4608:4608 + HALF]
        U = YTf[:, 4096:8192].rearrange("p (g l c) -> p g l c", g=G, l=L)
        KTS = YTf[:, 2048:2048 + HALF]
        WBs = WB[:, :].rearrange("p (s k c) -> p s k c", s=2, k=K)
        RWT = wa(12288, K, E)
        RB = wa(12544, E)
        MTM = wa(15300, L, E)
        LG = wa(12576, L, E)
        TV = wa(12832, L, 8)
        TIu = wa(12896, L, 8).bitcast(U32)
        TIf = wa(12960, L, 8)
        GW = sm[:, 176:208].rearrange("p (l j) -> p l j", l=L)
        IO, IOP = sm[:, 208:240], sm[:, 240:241]
        TOKI, IOI = sm[:, 241:249].bitcast(I32), IOI_[:, :]
        MXT = sm[:, 104:112]
        OH = wa(13088, TOPK, L * E)
        MS = wa(14112, L, E)
        GF = wa(14368, L, E)
        CU = wa(14624, L + 1, E)
        SL = wa(14912, L * E)
        LE = wa(14912, 2, P)[0:E]
        CNT, NTI, PEN, PST = (wa(15168 + 32 * n, E) for n in range(4))
        OHS = YTf[:, 0:1024].rearrange("p (j n) -> p j n", j=TOPK)
        TRI = YTf[:, 1024:1152]
        POSf = YTf[:, 1152:1152 + 32]
        POS = YTf[:, 1184:1216].bitcast(I32)
        ITE = YTf[:, 1224:1227]
        IT1, IT2, IT3 = (YTf[:, 1228 + 32 * n:1260 + 32 * n] for n in range(3))
        ITM = YTf[0:1, 6720:6720 + 3 * P].bitcast(I32)
        POSY = YTf[:, 7104:7136].bitcast(I32)
        CX, IT4 = YTf[:, 7136:7168], YTf[:, 7424:7456]
        SLY = YTf[:, 7168:7424]
        NROW = 2 * (ITEMS + 1)
        TBI = YTf[:, 1580:1708].bitcast(I32)
        TBF = YTf[:, 1708:1836]
        IDX = YTf[:, 7456:7456 + P].bitcast(I32)
        GTT = YTf[:, 1964:1964 + T]
        BDN = YTf[:, 2988:2988 + D]
        IDC = YTf[:, 7584:7586].bitcast(I32)
        BGC = YTf[:, 7586:7586 + 2 * FT]
        GA = YTf[:, 4160:4160 + 2 * W].rearrange("p (b n) -> p b n", b=2)
        SI = YTf[:, 4672:4672 + 2 * W].rearrange("p (b n) -> p b n", b=2)
        UP = YTf[:, 5184:5184 + 2 * W].rearrange("p (b n) -> p b n", b=2)
        FG = YTf[:, 5696:5696 + D]
        GUW = WA[:, :].rearrange("p (s h k c) -> p s h k c", s=4, h=2, k=K)
        CB = WA[:, :].rearrange("p (b j d) -> p b j d", b=4, j=TOPK)

        xn_rows = nc.dram_tensor("xn_rows", (T, D), F32).ap()
        y_rows = nc.dram_tensor("y_rows", (T * TOPK + W, D), F32).ap()
        slot_tok = nc.dram_tensor("slot_tok", (NROW * P, 1), I32).ap()

        V_MIX, V_XA, V_MEM, V_FFN, V_BA, V_BX, V_LAM, V_CW, V_CB = 0, 8, 16, 24, 32, 36, 40, 44, 60
        V_LR, V_LI, V_LD, V_GLB = 64, 80, 96, 112

        order = [("vec",)] + [("xt", l, h) for l in range(L) for h in range(2)]
        order += [("bgu",), ("cre",), ("cim",)]
        order += [("u", l) for l in range(L)]

        def rg(kind, ct):
            return [(kind, ct, h) for h in range(2)]

        def zz(ct):
            return [("z", ct, w, h) for w in range(2) for h in range(2)]

        order += rg("xr", 0) + rg("g", 0)
        order += [("ktap", b) for b in range(2)] + [("em", n) for n in range(8)]
        for ct in range(CT):
            if ct + 1 < CT:
                order += rg("xr", ct + 1)
            order += zz(ct)
            if ct + 1 < CT:
                order += rg("g", ct + 1)
        order += [("ut", n) for n in range(8)]
        for n in range(4):
            order += [("s", 0, n), ("s", 1, n)]
        order += [("y", n) for n in range(8)]
        order += [("zt", cb, h) for cb in range(CT) for h in range(2)]
        order += [("glu", cb, h) for cb in range(CT) for h in range(2)]
        order += [("wo1", c, l) for c in range(2) for l in range(L)]
        order += [("mt", m, h) for m in range(MT) for h in range(2)]
        order += [("kk", j) for j in range(K)] + [("vv", c, m) for c in range(2) for m in range(MT)]
        order += [("xt2", l, h) for l in range(L) for h in range(2)]
        order += [("q", j, h) for j in range(K) for h in range(2)]
        att = [(l, hp) for l in range(L) for hp in range(2)]
        LEAD = 3
        for n in range(len(att) + LEAD):
            if n < len(att):
                order.append(("sc",) + att[n])
            if n >= LEAD:
                order.append(("pt",) + att[n - LEAD])
        order += [("ot", h, d, f) for h in range(NH) for d in range(2) for f in range(2)]
        order += [("wo2", c, l) for c in range(2) for l in range(L)]
        for n in range(L + 2):
            order += [("xt3", n, h) for h in range(2) if n < L]
            order += [("rl", n - 1)] * (0 < n <= L) + [("rt", n - 2)] * (n >= 2)
        order += [("rank",), ("cnt",), ("itm",), ("gft", 0), ("gft", 1)]
        order += [("bd", l, c) for l in range(L) for c in range(2)]
        order += [("idx",)]
        number = {u: n for n, u in enumerate(order)}
        filled = [sem(f"bank{b}_filled") for b in range(8)]
        emptied = [sem(f"bank{b}_emptied") for b in range(8)]

        def bank(u):
            return PS[:, number[u] % 8, :]

        def wait_filled(eng, u):
            eng.wait_ge(filled[number[u] % 8], number[u] // 8 + 1)

        def emptied_by(u):
            return emptied[number[u] % 8]

        dve_step, act_step, pool_step = sem("dve_step"), sem("act_step"), sem("pool_step")
        steps = {}

        def link(eng, ins, s):
            steps[s.name] = steps.get(s.name, 0) + 1
            ins.then_inc(s, 1)
            eng.wait_ge(s, steps[s.name])

        def evac(eng, ins, u, own=False):
            s = emptied[number[u] % 8]
            ins.then_inc(s, 1)
            if own:
                eng.wait_ge(s, number[u] // 8 + 1)

        def unit_read(eng, u):
            eng.wait_ge(emptied[number[u] % 8], number[u] // 8 + 1)

        def units_read(eng, kind):
            for b in range(8):
                last = max((n for u, n in number.items() if u[0] == kind and n % 8 == b), default=None)
                if last is not None:
                    eng.wait_ge(emptied[b], last // 8 + 1)

        x_in = [sem(f"x_in{n}") for n in range(4)]
        vec_in, par_in, blk_in, mem_in = sem("vec_in"), sem("par_in"), sem("blk_in"), sem("mem_in")
        x_again, d_in, rt_in, zero_out = sem("x_again"), sem("d_in"), sem("rt_in"), sem("zero_out")
        w_in_s = [sem(f"wslot{s}_in") for s in range(2)]
        consts, ldt_ready, zeroed, eps_done = sem("consts"), sem("ldt_ready"), sem("zeroed"), sem("eps_done")
        ssq_done = [sem(f"ssq{n}_done") for n in range(5)]
        rstd_done = [sem(f"rstd{n}_done") for n in range(5)]
        xn_done = [sem(f"xn{n}_done") for n in range(4)]
        v_done, dt_done, ang_done, trig_done, rgc_done = (
            sem("v_done"), sem("dt_done"), sem("ang_done"), sem("trig_done"), sem("rgc_done"))
        bb_done, g_done, rot_done, f_done = sem("bb_done"), sem("g_done"), sem("rot_done"), sem("f_done")
        kts_done, mm_in, hp_done = sem("kts_done"), sem("mm_in"), sem("hp_done")
        glu_done, db_done, iota_done, y_zero = sem("glu_done"), sem("db_done"), sem("iota_done"), sem("y_zero")
        xr_zero, xc_done, rg_tp, rg_q, rg_sq, rg_done = (
            sem("xr_zero"), sem("xc_done"), sem("rg_tp"), sem("rg_q"), sem("rg_sq"), sem("rg_done"))
        h1_done, h2_done = sem("h1_done"), sem("h2_done")
        mx_done, exp_done, pn_done = sem("mx_done"), sem("exp_done"), sem("pn_done")
        xn_out, gexp_in, gexp_done, gf_done = sem("xn_out"), sem("gexp_in"), sem("gexp_done"), sem("gf_done")
        ms_done, pos_done, itm_done, ite_done = sem("ms_done"), sem("pos_done"), sem("itm_done"), sem("ite_done")
        scat, tb_in, tbf_done, idx_done = sem("scat"), sem("tb_in"), sem("tbf_done"), sem("idx_done")
        bdn_in, tri_done, fg_in, h3_done = sem("bdn_in"), sem("tri_done"), sem("fg_in"), sem("h3_done")
        gu_in = [sem(f"gu{s}_in") for s in range(4)]
        dn_in = [sem(f"dn{s}_in") for s in range(2)]
        dn_high, dn_split, hid_done = sem("dn_high"), sem("dn_split"), sem("hid_done")
        xg_in, xe_filled, xe_done, idc_done = sem("xg_in"), sem("xe_filled"), sem("xe_done"), sem("idc_done")
        gb_filled, gb_free, ga_done, si_done, ht_done = (
            sem("gb_filled"), sem("gb_free"), sem("ga_done"), sem("si_done"), sem("ht_done"))
        dn_used, y_done, y_out, bgc_done, ffn_step = (
            sem("dn_used"), sem("y_done"), sem("y_out"), sem("bgc_done"), sem("ffn_step"))
        gather_go, ys_free = sem("gather_go"), sem("ys_free")
        cb_in = [sem(f"cb{b}_in") for b in range(4)]
        comb_done, out_ready, out_sent = sem("comb_done"), sem("out_ready"), sem("out_sent")
        last_scaled, out_ready_dve = sem("last_scaled"), sem("out_ready_dve")

        def cols(name, c0):
            return A[name][:, c0:c0 + HALF].rearrange("(k p) c -> p k c", p=P)

        RGC = CT * P
        chunks = [("u", cols("w_in", 2 * RGC)), ("xr", cols("w_in", RGC)), ("g", cols("w_in", 0))]
        chunks += [(("o1", c), cols("w_out", c * HALF)) for c in range(2)]
        chunks += [(("kv", c), cols("xa_wkv", c * HALF)) for c in range(4)]
        chunks += [(("q", c), cols("xa_wq", c * HALF)) for c in range(2)]
        chunks += [(("o2", c), cols("xa_wo", c * HALF)) for c in range(2)]
        chunk_no = {name: n for n, (name, _) in enumerate(chunks)}

        def wslot(name):
            return WBs[:, chunk_no[name] % 2, :, :]

        block = ctx.enter_context(nc.Block())

        x_tok = A["x"].rearrange("b (p l) d -> p (b l) d", l=L)
        o_tok = out.rearrange("b (p l) d -> p (b l) d", l=L)

        def by_width(eng, n_i, item):
            with eng.If(n_i > 0):
                with eng.If(n_i > P):
                    with eng.If(n_i > 192):
                        item(W)
                    with eng.Else():
                        with eng.If(n_i > 160):
                            item(192)
                        with eng.Else():
                            item(160)
                with eng.Else():
                    item(P)

        @contextmanager
        def items(eng):
            with eng.Fori(0, ITEMS // GROUP) as b:
                with eng.If(item_tokens(eng, b * GROUP) > 0):
                    with eng.Fori(0, GROUP) as j:
                        yield b * GROUP + j

        def item_tokens(eng, i):
            return eng.value_load(ITM[0:1, bass.ds(i + P, 1)], min_val=0, max_val=W)

        def item_expert(eng, i):
            return eng.value_load(ITM[0:1, bass.ds(i, 1)], min_val=0, max_val=E - 1)

        @block.sync
        def _(sp):
            for n in range(4):
                if n == 1:
                    sp.wait_ge(vec_in, 16 * 13)
                sp.dma_start(H[:, 2 * n:2 * n + 2, :], x_tok[:, 2 * n:2 * n + 2, :]).then_inc(x_in[n], 16)
            bgu_rows = A["exp_b_gu"].rearrange("e (f p) -> (e f) p", p=P)
            for t in range(4):
                sp.dma_start(BGR[:, t, :], bgu_rows[t * P:(t + 1) * P, :]).then_inc(par_in, 16)
            for w, name in enumerate(("s5_c_re", "s5_c_im")):
                for b in range(2):
                    sp.dma_start(CRW[:, w, :, b, :],
                                  A[name].rearrange("(t g) c n -> (g c) t n", t=4)).then_inc(par_in, 16)
            for w, name in enumerate(("s5_b_re", "s5_b_im")):
                sp.dma_start(BRW[:, w, :, :], A[name].rearrange("(q b) n c -> (b n) q c", b=2)).then_inc(par_in, 16)
            sp.dma_start(DB, A["s5_d"].partition_broadcast(P)).then_inc(d_in, 16)
            sp.dma_start(wslot("u"), chunks[0][1]).then_inc(w_in_s[0], 16)
            sp.dma_start(wslot("xr"), chunks[1][1]).then_inc(w_in_s[1], 16)
            last_unit = {"u": ("u", L - 1), "xr": ("xr", CT - 1, 1), "g": ("g", CT - 1, 1)}
            for c in range(2):
                last_unit[("o1", c)] = ("wo1", c, L - 1)
                last_unit[("o2", c)] = ("wo2", c, L - 1)
                last_unit[("kv", c)] = ("kk", 4 * c + 3)
                last_unit[("kv", 2 + c)] = ("vv", c, MT - 1)
                last_unit[("q", c)] = ("q", 4 * c + 3, 1)
            for n in range(2, len(chunks)):
                wait_filled(sp, last_unit[chunks[n - 2][0]])
                sp.dma_start(WBs[:, n % 2, :, :], chunks[n][1]).then_inc(w_in_s[n % 2], 16)
                if n == 4:
                    wait_filled(sp, ("y", 7))
                    sp.dma_start(XR0, x_tok).then_inc(x_again, 16)
                    sp.dma_start(MEM, A["mem"].rearrange("b (m p) d -> p (b m) d", p=P)).then_inc(mem_in, 16)
            wait_filled(sp, ("ot", NH - 1, 1, 1))
            sp.dma_start(RWT, A["router_w"].rearrange("(k p) e -> p k e", p=P)).then_inc(rt_in, 16)
            sp.dma_start(RB, A["router_b"].partition_broadcast(P)).then_inc(rt_in, 16)
            for l in range(L):
                sp.wait_ge(xn_done[3], l + 1)
                sp.dma_start(xn_rows.rearrange("(p l) d -> p l d", l=L)[:, l, :], XR0[:, l, :]).then_inc(xn_out, 16)
            sp.dma_start(BDN[0:E, :], A["exp_b_down"]).then_inc(bdn_in, 16)
            sp.dma_start(FG, A["final_norm_g"].partition_broadcast(P)).then_inc(fg_in, 16)
            gu_v = A["exp_w_gu"].rearrange("e (k p) (h c) -> p e h k c", p=P, h=2)
            dn_v = A["exp_w_down"].rearrange("e (k p) d -> p e k d", p=P)

            def load_gate_up(s, e):
                for h in range(2):
                    sp.dma_start(GUW[:, s, h, :, :],
                                 gu_v[:, e, h, :, s * 256:(s + 1) * 256]
                                 .rearrange("p e k c -> p (e k) c")).then_inc(gu_in[s], 16)

            def load_down(s, e):
                sp.dma_start(DNW[:, s % 2, :, :],
                             dn_v[:, e, 2 * s:2 * s + 2, :].rearrange("p e k d -> p (e k) d")) \
                    .then_inc(dn_in[s % 2], 16)

            wait_filled(sp, ("xt3", L - 1, 1))
            sp.wait_ge(xn_out, 16 * L)
            for s in range(3):
                load_gate_up(s, slice(0, 1))
            for s in range(2):
                load_down(s, slice(0, 1))
            wait_filled(sp, ("gft", 1))
            sp.wait_ge(itm_done, 1)
            load_gate_up(3, slice(0, 1))
            sp.wait_ge(scat, 16 * TOPK * L)
            sp.dma_start(TBI[0:NROW, :], slot_tok.rearrange("(r p) o -> r (p o)", p=P)).then_inc(tb_in, 16)
            with items(sp) as i:
                with sp.If(item_tokens(sp, i) > 0):
                    e_i = item_expert(sp, i)
                    for s in (2, 3):
                        sp.wait_ge(dn_split, 8 * i + 2 * s + 2)
                        load_down(s, bass.ds(e_i, 1))
                with sp.If(item_tokens(sp, i + 1) > 0):
                    e_next = item_expert(sp, i + 1)
                    for s in range(4):
                        sp.wait_ge(gb_filled, 8 * i + 2 * s + 2)
                        load_gate_up(s, bass.ds(e_next, 1))
                    for s in range(2):
                        sp.wait_ge(dn_split, 8 * i + 2 * s + 10)
                        load_down(s, bass.ds(e_next, 1))
            for l in range(L):
                if l < POOL_TILES:
                    sp.wait_ge(out_ready, l + 1)
                else:
                    sp.wait_ge(out_ready_dve, l + 1 - POOL_TILES)
                sp.dma_start(o_tok[:, l, :], H[:, l, :]).then_inc(out_sent, 16)
            sp.wait_ge(out_sent, 16 * L)

        @block.tensor
        def _(pe):
            def begin(u):
                n = number[u]
                if n >= 8:
                    pe.wait_ge(emptied[n % 8], n // 8)
                return PS[:, n % 8, :]

            def end(u, ins):
                ins.then_inc(filled[number[u] % 8], 1)

            def weights(name):
                n = chunk_no[name]
                pe.wait_ge(w_in_s[n % 2], 16 * (n // 2 + 1))
                return WBs[:, n % 2, :, :]

            def mm(o, a, b, k, n):
                return nc.tensor.matmul(o, a, b, start=(k == 0), stop=(k == n - 1))

            pe.wait_ge(consts, 2)
            pe.wait_ge(vec_in, 16 * 13)
            pe.wait_ge(ldt_ready, 1)
            o = begin(("vec",))
            end(("vec",), nc.tensor.transpose(o[:, 0:116], RW1[0:116, :], ident[0:116, 0:116]))
            def tile_transposes(kind, l, norm, src):
                pe.wait_ge(xn_done[norm], l + 1)
                for h in range(2):
                    o = begin((kind, l, h))
                    for k in range(4):
                        c = (4 * h + k) * P
                        ins = nc.tensor.transpose(o[:, k * P:(k + 1) * P], src[:, l, c:c + P], ident[:])
                    end((kind, l, h), ins)

            def transposes(kind, norm, src):
                for l in range(L):
                    tile_transposes(kind, l, norm, src)

            transposes("xt", 0, YT)
            pe.wait_ge(par_in, 16 * 10)
            o = begin(("bgu",))
            for r in range(4):
                ins = nc.tensor.transpose(o[:, r * P:(r + 1) * P], BGR[:, r, :], ident[:])
            end(("bgu",), ins)
            for w, u in enumerate((("cre",), ("cim",))):
                o = begin(u)
                for r in range(4):
                    ins = nc.tensor.transpose(o[:, r * P:(r + 1) * P],
                                              CRW[:, w, r, :, :].rearrange("p a b -> p (a b)"), ident[:])
                end(u, ins)
            w = weights("u")
            units_read(pe, "xt")
            for l in range(L):
                o = begin(("u", l))
                for k in range(K):
                    ins = mm(o, XT[:, k, l * P:(l + 1) * P], w[:, k, :], k, K)
                end(("u", l), ins)

            def proj(kind, ct):
                w = weights(kind)
                for h in range(2):
                    o = begin((kind, ct, h))
                    for k in range(K):
                        ins = mm(o, w[:, k, ct * P:(ct + 1) * P], XT[:, k, h * HALF:(h + 1) * HALF], k, K)
                    end((kind, ct, h), ins)

            def gates(ct):
                pe.wait_ge(xc_done, ct + 1)
                for w2, wt in enumerate((BA, BX)):
                    for h in range(2):
                        o = begin(("z", ct, w2, h))
                        end(("z", ct, w2, h), mm(o, wt[:, ct, :], XC[:, h * HALF:(h + 1) * HALF], 0, 1))

            proj("xr", 0)
            proj("g", 0)
            pe.wait_ge(g_done, 1)
            for b in range(2):
                r = slice(NS * b, NS * b + NS)
                o = begin(("ktap", b))
                for q in range(Q):
                    for w2 in range(2):
                        ins = mm(o[:, q * SC:(q + 1) * SC],
                                 GM[r, w2, q, :, :].rearrange("p a b -> p (a b)"), CC[r, w2, q, :], w2, 2)
                end(("ktap", b), ins)
            for n in range(8):
                o = begin(("em", n))
                for j in range(4):
                    w2, q = divmod(4 * n + j, Q)
                    ins = nc.tensor.transpose(o[:, j * P:(j + 1) * P],
                                              GM[:, w2, q, :, :].rearrange("p a b -> p (a b)"), ident[:])
                end(("em", n), ins)
            pe.wait_ge(blk_in, 16 * 12)
            for ct in range(CT):
                if ct + 1 < CT:
                    proj("xr", ct + 1)
                gates(ct)
                if ct + 1 < CT:
                    proj("g", ct + 1)

            units_read(pe, "u")
            for n in range(8):
                o = begin(("ut", n))
                for j in range(4):
                    g = 4 * n + j
                    ins = nc.tensor.transpose(o[:, j * P:(j + 1) * P], U[:, g, :, :].rearrange("p a b -> p (a b)"), ident[:])
                end(("ut", n), ins)
            units_read(pe, "em")
            units_read(pe, "ut")
            for n in range(4):
                for w2 in range(2):
                    o = begin(("s", w2, n))
                    for j in range(4):
                        q = 4 * n + j
                        for b in range(2):
                            r = slice(NS * b, NS * b + NS)
                            ins = mm(o[r, j * P:(j + 1) * P], EM[:, w2, q, r], UT[:, 2 * q + b, :], 0, 1)
                    end(("s", w2, n), ins)
            pe.wait_ge(mm_in, 16 * L)
            for n in range(8):
                pe.wait_ge(hp_done, n // 2 + 1)
                pe.wait_ge(f_done, n // 4 + 1)
                o = begin(("y", n))
                for j in range(4):
                    g = 8 * (n // 2) + 2 * j + n % 2
                    r = slice(NS * (g % 2), NS * (g % 2) + NS)
                    oo = o[:, j * P:(j + 1) * P]
                    mm(oo, UT[:, g, :], MM[:, :, g * SC:(g + 1) * SC], 0, 3)
                    for w2 in range(2):
                        ins = mm(oo, HP[r, w2, g // 2, :],
                                 FM[r, w2, g // 2, :, :].rearrange("p a b -> p (a b)"), w2 + 1, 3)
                end(("y", n), ins)
            units_read(pe, "y")
            for cb in range(CT):
                for h in range(2):
                    o = begin(("zt", cb, h))
                    for j in range(4):
                        ins = nc.tensor.transpose(o[:, j * P:(j + 1) * P],
                                                  YTK[:, 4 * h + j, cb * P:(cb + 1) * P], ident[:])
                    end(("zt", cb, h), ins)
            units_read(pe, "zt")
            for cb in range(CT):
                for h in range(2):
                    o = begin(("glu", cb, h))
                    end(("glu", cb, h), mm(o, BG[:, cb, :], YT[:, CT + cb, h * HALF:(h + 1) * HALF], 0, 1))
            pe.wait_ge(glu_done, 2 * CT)
            pe.wait_ge(rg_done, CT)

            def out_proj(kind, name):
                for c in range(2):
                    w = weights((name, c))
                    for l in range(L):
                        o = begin((kind, c, l))
                        for k in range(K):
                            ins = mm(o, YT[:, k, l * P:(l + 1) * P], w[:, k, :], k, K)
                        end((kind, c, l), ins)

            out_proj("wo1", "o1")
            for m in range(MT):
                pe.wait_ge(xn_done[1], m + 1)
                for h in range(2):
                    o = begin(("mt", m, h))
                    for k in range(4):
                        c = (4 * h + k) * P
                        ins = nc.tensor.transpose(o[:, k * P:(k + 1) * P], MEM[:, m, c:c + P], ident[:])
                    end(("mt", m, h), ins)
            units_read(pe, "mt")
            for c in range(2):
                w = weights(("kv", c))
                for j in range(4):
                    o = begin(("kk", 4 * c + j))
                    for k in range(K):
                        ins = mm(o[:, 0:ML], w[:, k, j * P:(j + 1) * P], MEMT[:, k, :], k, K)
                    end(("kk", 4 * c + j), ins)
            for c in range(2):
                w = weights(("kv", 2 + c))
                for m in range(MT):
                    o = begin(("vv", c, m))
                    for k in range(K):
                        ins = mm(o, MEMT[:, k, m * P:(m + 1) * P], w[:, k, :], k, K)
                    end(("vv", c, m), ins)
            transposes("xt2", 2, XR0)
            units_read(pe, "xt2")
            for c in range(2):
                w = weights(("q", c))
                for j in range(4):
                    for h in range(2):
                        u = ("q", 4 * c + j, h)
                        o = begin(u)
                        for k in range(K):
                            ins = mm(o, w[:, k, j * P:(j + 1) * P], XT[:, k, h * HALF:(h + 1) * HALF], k, K)
                        end(u, ins)
            for kind in ("q", "kk", "vv"):
                units_read(pe, kind)
            for n in range(len(att) + LEAD):
                if n < len(att):
                    l, hp = att[n]
                    o = begin(("sc", l, hp))
                    for hh in range(2):
                        for d in range(2):
                            k = 2 * (2 * hp + hh) + d
                            ins = mm(o[:, hh * ML:(hh + 1) * ML], YT[:, k, l * P:(l + 1) * P], KT[:, k, :], d, 2)
                    end(("sc", l, hp), ins)
                if n >= LEAD:
                    l, hp = att[n - LEAD]
                    pe.wait_ge(pn_done, n - LEAD + 1)
                    o = begin(("pt", l, hp))
                    for hh in range(2):
                        for m in range(MT):
                            ins = nc.tensor.transpose(o[:, (2 * hh + m) * P:(2 * hh + m + 1) * P],
                                                      PP[:, (n - LEAD) % 2, hh, m * P:(m + 1) * P], ident[:])
                    end(("pt", l, hp), ins)
            units_read(pe, "pt")
            for h in range(NH):
                for d in range(2):
                    for f in range(2):
                        o = begin(("ot", h, d, f))
                        for m in range(MT):
                            c = h * HD + d * P
                            ins = mm(o, VV[:, m, c:c + P], PT[:, h, m, f * HALF:(f + 1) * HALF], m, MT)
                        end(("ot", h, d, f), ins)
            units_read(pe, "ot")
            out_proj("wo2", "o2")
            for n in range(L + 2):
                if n < L:
                    tile_transposes("xt3", n, 3, XR0)
                if 0 < n <= L:
                    l = n - 1
                    if l == 0:
                        pe.wait_ge(rt_in, 32)
                    for h in range(2):
                        unit_read(pe, ("xt3", l, h))
                    o = begin(("rl", l))
                    for k in range(K):
                        ins = mm(o[0:E, 0:P], RWT[:, k, :], XT[:, k, l * P:(l + 1) * P], k, K)
                    end(("rl", l), ins)
                if n >= 2:
                    l = n - 2
                    unit_read(pe, ("rl", l))
                    o = begin(("rt", l))
                    end(("rt", l), nc.tensor.transpose(o[:, 0:E], LE[:, l % 2, :], ident[0:E, 0:E]))
            pe.wait_ge(ms_done, 1)
            pe.wait_ge(tri_done, 1)
            o = begin(("rank",))
            mm(o[:, 0:L * E], TRI, MS.rearrange("p a b -> p (a b)"), 0, 2)
            end(("rank",), mm(o[:, 0:L * E], ones[:], CU[:, 0:L, :].rearrange("p a b -> p (a b)"), 1, 2))
            o = begin(("cnt",))
            end(("cnt",), mm(o[:, 0:E], ones[:], CU[:, L, :], 0, 1))
            pe.wait_ge(ite_done, 1)
            o = begin(("itm",))
            mm(o[0:1, 0:P], ITE[:, 0:1], ident[:], 0, 1)
            mm(o[0:1, P:2 * P], ITE[:, 1:2], ident[:], 0, 1)
            end(("itm",), mm(o[0:1, 2 * P:3 * P], ITE[:, 2:3], ident[:], 0, 1))
            pe.wait_ge(gf_done, 1)
            for h in range(2):
                o = begin(("gft", h))
                for j in range(4):
                    ins = nc.tensor.transpose(o[0:E, j * P:(j + 1) * P], GF[:, 4 * h + j, :], ident[:])
                end(("gft", h), ins)
            pe.wait_ge(bdn_in, 16)
            units_read(pe, "gft")
            for l in range(L):
                for c in range(2):
                    o = begin(("bd", l, c))
                    end(("bd", l, c), mm(o, GTT[0:E, l * P:(l + 1) * P], BDN[0:E, c * HALF:(c + 1) * HALF], 0, 1))
            pe.wait_ge(tbf_done, 1)
            o = begin(("idx",))
            end(("idx",), nc.tensor.transpose(o[:, 0:NROW], TBF[0:NROW, :], ident[0:NROW, 0:NROW]))
            for b in range(8):
                last = max(n for n in number.values() if n % 8 == b)
                pe.wait_ge(emptied[b], last // 8 + 1)
            pe.sem_inc(dn_used, 4)
            pe.wait_ge(itm_done, 1)

            def item_transposes(kp):
                o = PS[:, 2 + kp % 2, :].rearrange("p (k s) -> p k s", k=2)
                for kk in range(2):
                    for t in range(2):
                        c = (2 * kp + kk) * P
                        ins = nc.tensor.transpose(o[:, kk, t * P:(t + 1) * P], XG[:, t, c:c + P], ident[:])
                return ins

            pe.wait_ge(xg_in, 32)
            for kp in range(K // 2):
                if kp >= 2:
                    pe.wait_ge(xe_done, kp - 1)
                item_transposes(kp).then_inc(xe_filled, 1)
            pe.wait_ge(xe_done, K // 2)
            with items(pe) as i:
                n_i = item_tokens(pe, i)

                def item(n):
                    def gate_up(f):
                        s, f2 = divmod(f, 2)
                        if f2 == 0:
                            pe.wait_ge(gu_in[s], 32 * i + 32)
                        pe.wait_ge(gb_free, 8 * i + f + 1)
                        for hh in range(2):
                            for k in range(K):
                                ins = mm(PS[:, f % 2, hh * W:hh * W + n],
                                         GUW[:, s, hh, k, f2 * P:(f2 + 1) * P], XE[:, k, 0:n], k, K)
                        ins.then_inc(gb_filled, 1)

                    def down(k):
                        pe.wait_ge(dn_split, 8 * i + k + 5)
                        pe.wait_ge(ht_done, 8 * i + k + 1)
                        for t in range((n + P - 1) // P):
                            m = min(P, n - t * P)
                            for r, (hx, wx) in enumerate(((HTH, DNH), (HTL, DNH), (HTH, DNL))):
                                for c in range(2):
                                    ins = mm(PS[0:m, 4 + 2 * t + c, :], hx[:, k, t * P:t * P + m],
                                             wx[:, k % 4, c * HALF:(c + 1) * HALF], 3 * k + r, 3 * FT)
                        ins.then_inc(dn_used, 1)

                    def next_columns(kp):
                        if kp >= 2:
                            pe.wait_ge(xe_done, 4 * i + 3 + kp)
                        item_transposes(kp).then_inc(xe_filled, 1)

                    for f in range(FT - 1):
                        gate_up(f)
                    pe.wait_ge(xg_in, 32 * i + 64)
                    next_columns(0)
                    next_columns(1)
                    gate_up(FT - 1)
                    pe.wait_ge(y_done, i + 1)
                    down(0)
                    down(1)
                    next_columns(2)
                    next_columns(3)
                    for k in range(2, FT):
                        down(k)
                    pe.wait_ge(xe_done, 4 * i + 8)

                by_width(pe, n_i, item)

        @block.scalar
        def _(act):
            def a(dst, src, func, s=act_step, **kw):
                link(act, nc.scalar.activation(dst, src, func, **kw), s)

            def copy_unit(u, dst):
                wait_filled(act, u)
                evac(act, nc.scalar.copy(dst, bank(u)), u)

            rows = [("norm_mix_g", V_MIX), ("norm_xa_g", V_XA), ("mem_norm_g", V_MEM), ("norm_ffn_g", V_FFN),
                    ("rg_ba", V_BA), ("rg_bx", V_BX), ("rg_lambda", V_LAM), ("conv_b", V_CB), ("s5_glu_b", V_GLB)]
            for name, r in rows:
                n = A[name].shape[0] // P
                act.dma_start(RW1[r:r + n, :], A[name].rearrange("(n p) -> n p", p=P)).then_inc(vec_in, 16)
            act.dma_start(RW1[V_CW:V_CW + CW * CT, :],
                          A["conv_w"].rearrange("k (n p) -> (k n) p", p=P)).then_inc(vec_in, 16)
            for name, r in (("s5_lambda_re", V_LR), ("s5_lambda_im", V_LI)):
                act.dma_start(RW1[r:r + Q, :], A[name].rearrange("(q b) n -> q (b n)", b=2)).then_inc(vec_in, 16)
            act.dma_start(LDT[V_LD:V_LD + Q, :], A["s5_log_dt"].rearrange("(q b) -> q b", b=2)).then_inc(vec_in, 16)
            def norm(n, l, src, dst, c0, count=1):
                a(dst, src, ACT.Square, accum_out=sm[:, c0:c0 + 1])
                a(sm[:, c0 + 8:c0 + 9], sm[:, c0:c0 + 1], ACT.Sqrt, bias=sm[:, 127:128], scale=1.0 / D, s=ssq_done[n])
                act.wait_ge(rstd_done[n], l + 1)
                a(dst, src, ACT.Copy, scale=sm[:, c0 + 16:c0 + 17], s=xn_done[n])

            act.wait_ge(eps_done, 1)
            for l in range(L):
                if l % 2 == 0:
                    act.wait_ge(x_in[l // 2], 16)
                norm(0, l, H[:, l, :], YT[:, l, :], l)
            act.wait_ge(zeroed, 3)
            for t, name in ((BA, "rg_wa"), (BX, "rg_wx")):
                for b in range(2):
                    act.dma_start(t[64 * b:64 * b + 64, :, 64 * b:64 * b + 64],
                                  A[name].rearrange("(c b) i j -> b i c j", b=2)[b]).then_inc(blk_in, 16)
            for b in range(8):
                act.dma_start(BG[SC * b:SC * (b + 1), :, SC * b:SC * (b + 1)],
                              A["s5_glu_w"].rearrange("(c b) i j -> b i c j", b=8)[b]).then_inc(blk_in, 16)
            act.wait_ge(v_done, 1)
            a(sm[:, 24:40], V[:, V_LD:V_LD + Q], ACT.Exp, s=dt_done)
            act.wait_ge(ang_done, 3)
            a(sm[:, 40:56], sm[:, 40:56], ACT.Exp)
            a(sm[:, 88:92], sm[:, 88:92], ACT.Exp)
            a(sm[:, 56:72], sm[:, 56:72], ACT.Sin)
            a(sm[:, 72:88], sm[:, 72:88], ACT.Sin, s=trig_done)
            for l in range(L):
                wait_filled(act, ("u", l))
                evac(act, nc.scalar.copy(U[:, :, l, :], bank(("u", l)).rearrange("p (g c) -> p g c", g=G)), ("u", l))

            def xr(ct):
                act.wait_ge(xr_zero, 1)
                if ct:
                    act.wait_ge(xc_done, ct)
                for h in range(2):
                    u = ("xr", ct, h)
                    wait_filled(act, u)
                    dst = XRg[:, 3:3 + T].rearrange("p (k l) -> p l k", l=L)[:, 4 * h:4 * h + 4, :]
                    evac(act, nc.scalar.copy(dst, bank(u).rearrange("p (l k) -> p l k", l=4)), u)

            def gate(ct):
                if ct >= 2:
                    act.wait_ge(rg_done, ct - 1)
                for h in range(2):
                    u = ("g", ct, h)
                    wait_filled(act, u)
                    dst = GT[:, ct % 2, :].rearrange("p (k l) -> p l k", l=L)[:, 4 * h:4 * h + 4, :]
                    evac(act, nc.scalar.activation(dst, bank(u).rearrange("p (l k) -> p l k", l=4),
                                                   ACT.Gelu_apprx_tanh), u)

            def rg_gates(ct):
                if ct:
                    act.wait_ge(rg_done, ct)
                for w, (t, c) in enumerate(((TH, 0), (TI, 4))):
                    for h in range(2):
                        u = ("z", ct, w, h)
                        wait_filled(act, u)
                        evac(act, nc.scalar.activation(t[:, h * HALF:(h + 1) * HALF], bank(u), ACT.Tanh, scale=0.5,
                                                       bias=sm[:, 92 + c + ct:93 + c + ct]), u, own=True)
                a(TH, TH, ACT.Tanh, bias=sm[:, 100 + ct:101 + ct], scale=sm[:, 100 + ct:101 + ct], s=rg_tp)
                act.wait_ge(rg_q, ct + 1)
                a(TH, TH, ACT.Sqrt, s=rg_sq)

            xr(0)
            gate(0)
            for n in range(8):
                copy_unit(("em", n), EM.rearrange("p a b c -> p (a b c)")[:, n * HALF:(n + 1) * HALF])
            act.wait_ge(rgc_done, 1)
            for ct in range(CT):
                if ct + 1 < CT:
                    xr(ct + 1)
                rg_gates(ct)
                if ct + 1 < CT:
                    gate(ct + 1)
            for n in range(8):
                copy_unit(("ut", n), XTf[:, n * HALF:(n + 1) * HALF])
            for n in range(8):
                u = ("y", n)
                wait_filled(act, u)
                dst = YTK[:, :, (n // 2) * 128:(n // 2) * 128 + 128].rearrange("p l (g b c) -> p b g l c", g=4, b=2)
                evac(act, nc.scalar.copy(dst[:, n % 2], bank(u).rearrange("p (g l c) -> p g l c", g=4, l=L)), u)
            for cb in range(CT):
                for h in range(2):
                    u = ("zt", cb, h)
                    wait_filled(act, u)
                    evac(act, nc.scalar.activation(YT[:, CT + cb, h * HALF:(h + 1) * HALF], bank(u),
                                                   ACT.Gelu_apprx_tanh), u)
            for n in range(2 * CT):
                cb, h = divmod(n, 2)
                u = ("glu", cb, h)
                wait_filled(act, u)
                if n >= 2:
                    act.wait_ge(glu_done, n - 1)
                evac(act, nc.scalar.activation(SG[:, n % 2, :], bank(u), ACT.Sigmoid,
                                               bias=V[:, V_GLB + cb:V_GLB + cb + 1]), u)
            act.wait_ge(mem_in, 16)
            for m in range(MT):
                a(MEMT.rearrange("p k s -> p (k s)")[:, m * D:(m + 1) * D], MEM[:, m, :], ACT.Square,
                  accum_out=sm[:, 104 + m:105 + m])
                a(sm[:, 112 + m:113 + m], sm[:, 104 + m:105 + m], ACT.Sqrt, bias=sm[:, 127:128], scale=1.0 / D,
                  s=ssq_done[1])
                act.wait_ge(rstd_done[1], m + 1)
                a(MEM[:, m, :], MEM[:, m, :], ACT.Copy, scale=sm[:, 120 + m:121 + m], s=xn_done[1])
            for j in range(K):
                u = ("kk", j)
                wait_filled(act, u)
                evac(act, nc.scalar.copy(KT[:, j, :], bank(u)[:, 0:ML]), u)
            for c in range(2):
                for m in range(MT):
                    copy_unit(("vv", c, m), VV[:, m, c * HALF:(c + 1) * HALF])
            for l in range(L):
                act.wait_ge(h1_done, L + l + 1)
                norm(2, l, H[:, l, :], XR0[:, l, :], l)
            for j in range(K):
                for h in range(2):
                    copy_unit(("q", j, h), YT[:, j, h * HALF:(h + 1) * HALF])
            for n, (l, hp) in enumerate(att):
                u = ("sc", l, hp)
                act.wait_ge(mx_done, n + 1)
                if n >= 2:
                    wait_filled(act, ("pt",) + att[n - 2])
                b = n % 2
                for hh in range(2):
                    ins = nc.scalar.activation(PP[:, b, hh, :], bank(u)[:, hh * ML:(hh + 1) * ML], ACT.Exp,
                                               bias=sm[:, 24 + 2 * b + hh:25 + 2 * b + hh], scale=HD ** -0.5,
                                               accum_out=sm[:, 28 + 2 * b + hh:29 + 2 * b + hh])
                    if hh == 0:
                        ins.then_inc(exp_done, 1)
                evac(act, ins, u, own=True)
                act.sem_inc(exp_done, 1)
            for h in range(NH):
                for d in range(2):
                    for f in range(2):
                        copy_unit(("ot", h, d, f), YT[:, 2 * h + d, f * HALF:(f + 1) * HALF])
            for l in range(L):
                act.wait_ge(h2_done, L + l + 1)
                norm(3, l, H[:, l, :], XR0[:, l, :], l)
            act.wait_ge(gexp_in, 1)
            a(GW, GW, ACT.Exp, s=gexp_done)
            for h in range(2):
                u = ("gft", h)
                wait_filled(act, u)
                evac(act, nc.scalar.copy(GTT[0:E, h * HALF:(h + 1) * HALF], bank(u)[0:E, :]), u)

            def pair(kp, count):
                act.wait_ge(xe_filled, count)
                o = PS[:, 2 + kp % 2, :].rearrange("p (k s) -> p k s", k=2)
                for kk in range(2):
                    k = 2 * kp + kk
                    ins = nc.scalar.activation(XE[:, k, :], o[:, kk, :], ACT.Copy, scale=V[:, V_FFN + k:V_FFN + k + 1])
                ins.then_inc(xe_done, 1)

            act.wait_ge(itm_done, 1)
            for kp in range(4):
                pair(kp, kp + 1)
            act.sem_inc(y_done, 1)
            with items(act) as i:
                n_i = item_tokens(act, i)

                def high(k):
                    act.wait_ge(dn_in[k // 2 % 2], 32 * i + 16 * (k // 4) + 16)
                    act.wait_ge(dn_used, 8 * i + k + 1)
                    nc.scalar.copy(DNH[:, k % 4, :], DNW[:, k // 2 % 2, k % 2, :]).then_inc(dn_high, 1)

                def item(n):
                    for f in range(FT):
                        act.wait_ge(ga_done, 8 * i + f + 1)
                        nc.scalar.activation(SI[:, f % 2, 0:n], GA[:, f % 2, 0:n], ACT.Sigmoid, scale=ALPHA) \
                            .then_inc(si_done, 1)
                        if f < 4:
                            high(f)
                    pair(0, 4 * i + 5)
                    pair(1, 4 * i + 6)
                    high(4)
                    high(5)
                    pair(2, 4 * i + 7)
                    pair(3, 4 * i + 8)
                    high(6)
                    high(7)
                    act.wait_ge(dn_used, 8 * i + 12)
                    act.wait_ge(ys_free, i + 1)
                    for t in range((n + P - 1) // P):
                        m = min(P, n - t * P)
                        ins = nc.scalar.copy(YS[0:m, t, :],
                                             PS[0:m, 4 + 2 * t:6 + 2 * t, :].rearrange("p a b -> p (a b)"))
                    ins.then_inc(y_done, 1)

                by_width(act, n_i, item)
            for l in range(L):
                act.wait_ge(comb_done, l + 1)
                a(SQ[:, l % 2, :], H[:, l, :], ACT.Square, accum_out=sm[:, l:l + 1])
                a(sm[:, l + 8:l + 9], sm[:, l:l + 1], ACT.Sqrt, bias=sm[:, 127:128], scale=1.0 / D, s=ssq_done[4])
                if l < POOL_TILES:
                    act.wait_ge(rstd_done[4], l + 1)
                    a(H[:, l, :], H[:, l, :], ACT.Copy, scale=sm[:, l + 16:l + 17], s=last_scaled)

        @block.vector
        def _(dve):
            v = nc.vector

            def d(ins, s=dve_step):
                link(dve, ins, s)

            def tt(o, x, y, op, s=dve_step):
                d(v.tensor_tensor(o, x, y, op), s)

            def ts(o, x, c1, c2, op0, op1=ALU.bypass, s=dve_step):
                d(v.tensor_scalar(o, x, c1, c2, op0, op1) if c2 is not None else v.tensor_scalar(o, x, c1, None, op0), s)

            def stt(o, x, c, y, op0, op1, s=dve_step):
                d(v.scalar_tensor_tensor(out=o, in0=x, scalar=c, in1=y, op0=op0, op1=op1), s)

            mul, add, sub = ALU.mult, ALU.add, ALU.subtract
            d(v.memset(sm[:, 127:128], EPS), eps_done)
            dve.wait_ge(vec_in, 16 * 13)
            d(v.tensor_copy(RW1[V_LD:V_LD + Q, :].rearrange("p (b n) -> p b n", b=2),
                            LDT[V_LD:V_LD + Q, :].unsqueeze(2).to_broadcast([Q, 2, NS])), ldt_ready)
            wait_filled(dve, ("vec",))
            evac(dve, v.tensor_copy(V[:, :], bank(("vec",))[:, 0:116]), ("vec",), own=True)
            dve.sem_inc(v_done, 1)
            def rstd(n, l, c0):
                dve.wait_ge(ssq_done[n], l + 1)
                d(v.reciprocal(sm[:, c0 + 16:c0 + 17], sm[:, c0 + 8:c0 + 9]), rstd_done[n])

            def scaled(u, dst, g0, n=4):
                wait_filled(dve, u)
                evac(dve, v.tensor_tensor(dst, bank(u).rearrange("p (k s) -> p k s", k=n),
                                          V[:, g0:g0 + n].unsqueeze(2).to_broadcast([P, n, HALF // n]), mul), u)

            def norm_tiles(kind, n, gain):
                for l in range(L + 1):
                    if l < L:
                        rstd(n, l, l)
                    if l:
                        for h in range(2):
                            scaled((kind, l - 1, h), XT[:, 4 * h:4 * h + 4, (l - 1) * P:l * P], gain + 4 * h)

            norm_tiles("xt", 0, V_MIX)
            wait_filled(dve, ("bgu",))
            evac(dve, v.tensor_copy(BGU[:, :], bank(("bgu",))), ("bgu",))
            for w, u in enumerate((("cre",), ("cim",))):
                wait_filled(dve, u)
                o = bank(u).rearrange("p (q b c) -> p q b c", q=Q, b=2)
                d(v.tensor_scalar(CC[0:NS, w, :, :], o[0:NS, :, 0, :], -1.0 if w else 1.0, None, mul))
                evac(dve, v.tensor_scalar(CC[NS:P, w, :, :], o[NS:P, :, 1, :], -1.0 if w else 1.0, None, mul),
                     u, own=True)
            dve.wait_ge(xn_done[0], L)
            d(v.memset(XRg[:, 0:4], 0.0), xr_zero)

            dt, mg, sn, cs = sm[:, 24:40], sm[:, 40:56], sm[:, 56:72], sm[:, 72:88]
            mag8, uc, us = sm[:, 128:144], sm[:, 144:160], sm[:, 160:176]
            LR, LI = V[:, V_LR:V_LR + Q], V[:, V_LI:V_LI + Q]
            S = [SCR[:, n * Q:(n + 1) * Q] for n in range(14)]
            dve.wait_ge(dt_done, 1)
            tt(mg, dt, LR, mul, s=ang_done)
            ts(S[1], V[:, V_LI:V_LI + Q], 1.0, None, mul)
            tt(S[0], dt, LI, mul)
            ts(S[1], S[0], 1.0 / (2 * math.pi), None, mul)
            ts(S[1], S[1], 1.5 * 2 ** 23, None, add)
            ts(S[1], S[1], 1.5 * 2 ** 23, None, sub)
            C1 = 6.28125
            C2 = float(np.float32(2 * math.pi - C1) // 2.0 ** -22 * 2.0 ** -22)
            for c in (C1, C2, 2 * math.pi - C1 - C2):
                stt(S[0], S[1], -c, S[0], mul, add)
            BOUND = 3.1415925
            ts(sn, S[0], BOUND, -BOUND, ALU.min, ALU.max)
            ts(S[2], S[0], math.pi / 2, None, add)
            ts(S[3], S[2], math.pi, -2 * math.pi, ALU.is_gt, mul)
            tt(S[2], S[2], S[3], add)
            ts(cs, S[2], BOUND, -BOUND, ALU.min, ALU.max, s=ang_done)
            lam = V[:, V_LAM:V_LAM + CT]
            z = sm[:, 88:92]
            ts(z, lam, -1.0, None, mul)
            tt(z, z, lam, ALU.min, s=ang_done)
            dve.wait_ge(trig_done, 1)
            are, aim = PW[:, 0, :, 1], PW[:, 1, :, 1]
            tt(are, mg, cs, mul)
            tt(aim, mg, sn, mul)
            ts(S[4], are, 1.0, None, sub)
            tt(S[5], LR, LR, mul)
            tt(S[6], LI, LI, mul)
            tt(S[5], S[5], S[6], add)
            d(v.reciprocal(S[5], S[5]))
            tt(S[6], S[4], LR, mul)
            tt(S[7], aim, LI, mul)
            tt(S[6], S[6], S[7], add)
            tt(S[6], S[6], S[5], mul)
            tt(S[7], aim, LR, mul)
            tt(S[8], S[4], LI, mul)
            tt(S[7], S[7], S[8], sub)
            tt(S[7], S[7], S[5], mul)

            def wide(x):
                return x.unsqueeze(2).to_broadcast([P, Q, SC])

            B0, B1 = BRW[:, 0, :, :], BRW[:, 1, :, :]
            dve.wait_ge(par_in, 16 * 10)
            tt(BB[:, 0], wide(S[6]), B0, mul)
            tt(TMB, wide(S[7]), B1, mul)
            tt(BB[:, 0], BB[:, 0], TMB, sub)
            tt(BB[:, 1], wide(S[6]), B1, mul)
            tt(TMB, wide(S[7]), B0, mul)
            tt(BB[:, 1], BB[:, 1], TMB, add)
            d(v.memset(PW[:, 0, :, 0], 1.0))
            d(v.memset(PW[:, 1, :, 0], 0.0))

            def cmul(ore, oim, xr_, xi, yr, yi, t1, t2, s=dve_step):
                tt(t1, xr_, yr, mul)
                tt(t2, xi, yi, mul)
                tt(ore, t1, t2, sub)
                tt(t1, xr_, yi, mul)
                tt(t2, xi, yr, mul)
                tt(oim, t1, t2, add, s=s)

            for n in (1, 2, 4):
                x = [PW[:, r, :, 1:n + 1] for r in range(2)]
                y = [PW[:, r, :, n:n + 1].to_broadcast([P, Q, n]) for r in range(2)]
                t1 = SCR[:, 224:224 + Q * n].rearrange("p (q n) -> p q n", q=Q)
                t2 = SCR[:, 288:288 + Q * n].rearrange("p (q n) -> p q n", q=Q)
                cmul(PW[:, 0, :, n + 1:2 * n + 1], PW[:, 1, :, n + 1:2 * n + 1], x[0], x[1], y[0], y[1], t1, t2)
            for j in range(L):
                for r in range(2):
                    d(v.tensor_copy(QV[:, r, :, j], PW[:, r, :, L - 1 - j]))
            tt(S[9], mg, mg, mul)
            tt(S[9], S[9], S[9], mul)
            tt(mag8, S[9], S[9], mul)
            cmul(S[10], S[11], cs, sn, cs, sn, S[12], S[13])
            cmul(S[8], S[9], S[10], S[11], S[10], S[11], S[12], S[13])
            cmul(uc, us, S[8], S[9], S[8], S[9], S[12], S[13], s=bb_done)

            w, w2, ac = S[0][:, 0:CT], S[1][:, 0:CT], S[2][:, 0:CT]
            ts(w, z, 2.0, None, add)
            d(v.reciprocal(w, w))
            tt(w, w, z, mul)
            tt(w2, w, w, mul)
            ts(ac, w2, 1.0 / 19, 1.0 / 17, mul, add)
            for n in (15, 13, 11, 9, 7, 5, 3, 1):
                tt(ac, ac, w2, mul)
                ts(ac, ac, 1.0 / n, None, add)
            tt(ac, ac, w, mul)
            ts(w, lam, -1.0, 0.0, mul, ALU.max)
            stt(w, ac, 2.0, w, mul, add)
            ts(sm[:, 92:96], V[:, V_BA:V_BA + CT], 0.5, None, mul)
            ts(sm[:, 96:100], V[:, V_BX:V_BX + CT], 0.5, None, mul)
            ts(sm[:, 100:104], w, RG_C / 4, None, mul, s=rgc_done)

            def conv(ct):
                for h in range(2):
                    s = emptied[number[("xr", ct, h)] % 8]
                    dve.wait_ge(s, number[("xr", ct, h)] // 8 + 1)
                wk = [V[:, V_CW + k * CT + ct:V_CW + k * CT + ct + 1] for k in range(CW)]
                ts(XC, XRg[:, 0:T], wk[0], V[:, V_CB + ct:V_CB + ct + 1], mul, add)
                for k in range(1, CW):
                    stt(XC, XRg[:, k:k + T], wk[k], XC, mul, add, s=xc_done if k == CW - 1 else dve_step)

            conv(0)
            dve.wait_ge(db_done, 1)
            for b in range(2):
                u = ("ktap", b)
                wait_filled(dve, u)
                evac(dve, v.tensor_tensor(KTS.rearrange("p (q b c) -> p b q c", q=Q, b=2)[:, b],
                                          bank(u)[:, 0:Q * SC].rearrange("p (q c) -> p q c", q=Q),
                                          DB.rearrange("p (q b c) -> p b q c", q=Q, b=2)[:, b], add), u, own=True)
            dve.sem_inc(kts_done, 1)
            for ct in range(CT):
                dve.wait_ge(rg_tp, ct + 1)
                ts(QQ, TH, 1.0, None, add, s=rg_q)
                d(v.reciprocal(QQ, QQ))
                stt(TI, TI, 1.0, XC, add, mul)
                ts(XC, QQ, 2.0, -1.0, mul, add)
                dve.wait_ge(rg_sq, ct + 1)
                tt(QQ, QQ, TH, mul)
                d(v.memset(QQ[:, 0:1], 0.5))
                tt(TI, TI, QQ, mul)
                d(v.tensor_tensor_scan(QQ, XC, TI, 0.0, mul, add))
                if ct == 2:
                    dve.wait_ge(mm_in, 16 * L)
                for h in range(2):
                    dve.wait_ge(emptied[number[("g", ct, h)] % 8], number[("g", ct, h)] // 8 + 1)
                tt(YT[:, ct, :].rearrange("p (l k) -> p k l", l=L), QQ.rearrange("p (k l) -> p k l", l=L),
                   GT[:, ct % 2, :].rearrange("p (k l) -> p k l", l=L), mul, s=rg_done)
                if ct + 1 < CT:
                    conv(ct + 1)

            dve.wait_ge(rot_done, 1)
            d(v.memset(HP[:, :, :, 0], 0.0))
            for n in range(4):
                sl = slice(4 * n, 4 * n + 4)
                cr = RT[:, 0, sl, :].rearrange("p q k -> p (q k)")
                ci = RT[:, 1, sl, :].rearrange("p q k -> p (q k)")
                wait_filled(dve, ("s", 0, n))
                wait_filled(dve, ("s", 1, n))
                sre, sim = bank(("s", 0, n)), bank(("s", 1, n))
                ore, oim = (SR[:, r, sl, :].rearrange("p q k -> p (q k)") for r in range(2))
                tt(TA, cr, sre, mul)
                tt(TB, ci, sim, mul)
                tt(ore, TA, TB, add)
                d(v.tensor_tensor(TA, cr, sim, mul))
                evac(dve, v.tensor_tensor(TB, ci, sre, mul), ("s", 0, n), own=True)
                evac(dve, v.tensor_tensor(oim, TA, TB, sub), ("s", 1, n), own=True)
                for r in range(2):
                    for q in range(4 * n, 4 * n + 4):
                        d(v.tensor_tensor_scan(SR[:, r, q, :], mag8[:, q:q + 1].to_broadcast([P, P]),
                                               SR[:, r, q, :], 0.0, mul, add))
                if n == 0:
                    wait_filled(dve, ("s", 1, 3))
                e = P - 1
                cmul(HP[:, 0, sl, 1:], HP[:, 1, sl, 1:], RT[:, 0, sl, 0:e], RT[:, 1, sl, 0:e],
                     SR[:, 0, sl, 0:e], SR[:, 1, sl, 0:e], T1[:, sl, 0:e], T2[:, sl, 0:e], s=hp_done)
            for n in range(2 * CT):
                cb, h = divmod(n, 2)
                u = ("glu", cb, h)
                dve.wait_ge(emptied[number[u] % 8], number[u] // 8 + 1)
                y = YT[:, CT + cb, h * HALF:(h + 1) * HALF]
                tt(y, y, SG[:, n % 2, :], mul, s=glu_done)
            dve.wait_ge(x_again, 16)
            for c in range(2):
                for l in range(L):
                    u = ("wo1", c, l)
                    cc = slice(c * HALF, (c + 1) * HALF)
                    wait_filled(dve, u)
                    evac(dve, v.tensor_tensor(H[:, l, cc], bank(u), XR0[:, l, cc], add), u, own=True)
                    dve.sem_inc(h1_done, 1)
                if c == 0:
                    for m in range(MT):
                        rstd(1, m, 104 + m)
            for m in range(MT):
                for h in range(2):
                    scaled(("mt", m, h), MEMT[:, 4 * h:4 * h + 4, m * P:(m + 1) * P], V_MEM + 4 * h)
            norm_tiles("xt2", 2, V_XA)

            def maxima(n):
                u = ("sc",) + att[n]
                c = 24 + 2 * (n % 2)
                wait_filled(dve, u)
                d(v.tensor_reduce(MXT[:, 0:2], bank(u).rearrange("p (h m) -> p h m", h=2), AX.X, ALU.max))
                ts(sm[:, c:c + 2], MXT[:, 0:2], -HD ** -0.5, None, mul, s=mx_done)

            def normalise(n):
                b = n % 2
                dve.wait_ge(exp_done, 2 * n + 2)
                d(v.reciprocal(sm[:, 32:34], sm[:, 28 + 2 * b:30 + 2 * b]))
                tt(PP[:, b, :, :], PP[:, b, :, :], sm[:, 32:34].unsqueeze(2).to_broadcast([P, 2, ML]), mul, s=pn_done)

            def keep(n):
                l, hp = att[n]
                u = ("pt", l, hp)
                wait_filled(dve, u)
                evac(dve, v.tensor_copy(PT[:, 2 * hp:2 * hp + 2, :, l * P:(l + 1) * P],
                                        bank(u).rearrange("p (h m t) -> p h m t", h=2, m=MT)), u)

            for n in range(len(att) + LEAD):
                if n < len(att):
                    maxima(n)
                if 0 < n <= len(att):
                    normalise(n - 1)
                if n >= LEAD:
                    keep(n - LEAD)
            for c in range(2):
                for l in range(L):
                    u = ("wo2", c, l)
                    cc = slice(c * HALF, (c + 1) * HALF)
                    wait_filled(dve, u)
                    evac(dve, v.tensor_tensor(H[:, l, cc], bank(u), H[:, l, cc], add), u, own=True)
                    dve.sem_inc(h2_done, 1)
            for n in range(L + 3):
                if n < L:
                    rstd(3, n, n)
                if 0 < n <= L:
                    for h in range(2):
                        scaled(("xt3", n - 1, h), XT[:, 4 * h:4 * h + 4, (n - 1) * P:n * P], V_FFN + 4 * h)
                if 2 <= n < L + 2:
                    u = ("rl", n - 2)
                    wait_filled(dve, u)
                    evac(dve, v.tensor_copy(LE[:, n % 2, :], bank(u)[0:E, 0:P]), u)
                if n >= 3:
                    l = n - 3
                    if l == 0:
                        dve.wait_ge(rt_in, 32)
                    wait_filled(dve, ("rt", l))
                    evac(dve, v.tensor_tensor(LG[:, l, :], bank(("rt", l))[:, 0:E], RB, add), ("rt", l), own=True)
                    d(v.max(TV[:, l, :], LG[:, l, :]))
                    d(v.max_index(TIu[:, l, :], TV[:, l, :], LG[:, l, :]))

            d(v.tensor_copy(TIf, TIu))
            tt(GW, TV[:, :, 0:TOPK], TV[:, :, 0:1].to_broadcast([P, L, TOPK]), sub, s=gexp_in)
            dve.wait_ge(iota_done, 3)
            OH4 = OH.rearrange("p j (l e) -> p j l e", l=L)
            for j in range(TOPK):
                tt(OH4[:, j], TIf[:, :, j:j + 1].to_broadcast([P, L, E]), IO.unsqueeze(1).to_broadcast([P, L, E]),
                   ALU.is_equal)
            tt(MS, OH4[:, 0], OH4[:, 1], add)
            tt(MS, MS, OH4[:, 2], add)
            tt(MS, MS, OH4[:, 3], add)
            d(v.memset(CU[:, 0, :], 0.0))
            for l in range(L):
                tt(CU[:, l + 1, :], CU[:, l, :], MS[:, l, :], add, s=ms_done if l == L - 1 else dve_step)
            wait_filled(dve, ("rank",))
            wait_filled(dve, ("cnt",))
            evac(dve, v.tensor_copy(CNT, bank(("cnt",))[:, 0:E]), ("cnt",), own=True)
            ts(NTI, CNT, float(W), 1.0, ALU.is_gt, add)
            for n in range(2, T // W):
                ts(IT1, CNT, float(n * W), None, ALU.is_gt)
                tt(NTI, NTI, IT1, add)
            d(v.tensor_tensor_scan(PEN, ones[:, 0:E], NTI, 0.0, mul, add))
            tt(PST, PEN, NTI, sub)
            ts(IT1, PST, float(W), None, mul)
            evac(dve, v.tensor_tensor(SL.rearrange("p (l e) -> p l e", l=L),
                                      bank(("rank",))[:, 0:L * E].rearrange("p (l e) -> p l e", l=L),
                                      IT1.unsqueeze(1).to_broadcast([P, L, E]), add), ("rank",), own=True)
            tt(OHS, OH, SL.unsqueeze(1).to_broadcast([P, TOPK, L * E]), mul)
            d(v.tensor_reduce(POSf, OHS.rearrange("p j (l e) -> p (j l) e", l=L), AX.X, add))
            d(v.tensor_copy(POS, POSf), pos_done)
            dve.wait_ge(gexp_done, 1)
            d(v.tensor_reduce(MXT[:, 0:L], GW, AX.X, add))
            d(v.reciprocal(MXT[:, 0:L], MXT[:, 0:L]))
            tt(GW, GW, MXT[:, 0:L].unsqueeze(2).to_broadcast([P, L, TOPK]), mul)
            for j in range(TOPK):
                t = GF if j == 0 else MTM
                tt(t, OH4[:, j], GW[:, :, j:j + 1].to_broadcast([P, L, E]), mul)
                if j:
                    tt(GF, GF, MTM, add, s=gf_done if j == TOPK - 1 else dve_step)
            d(v.tensor_tensor_scan(CX, ones[:, 0:E], CNT, 0.0, mul, add))
            tt(CX, CX, CNT, sub)
            tt(IT2, CX, IT1, sub)
            tt(SLY.rearrange("p (l e) -> p l e", l=L), SL.rearrange("p (l e) -> p l e", l=L),
               IT2.unsqueeze(1).to_broadcast([P, L, E]), add)
            tt(OHS, OH, SLY.unsqueeze(1).to_broadcast([P, TOPK, L * E]), mul)
            d(v.tensor_reduce(POSf, OHS.rearrange("p j (l e) -> p (j l) e", l=L), AX.X, add))
            d(v.tensor_copy(POSY, POSf))
            tt(CNT, CNT, IT1, add)
            ts(IT2, PEN, IOP, None, ALU.is_le)
            ts(IT3, PST, IOP, None, ALU.is_le)
            d(v.tensor_reduce(ITE[:, 0:1], IT2, AX.X, add))
            ts(ITE[:, 0:1], ITE[:, 0:1], float(E - 1), None, ALU.min)
            tt(IT3, IT3, IT2, sub)
            d(v.tensor_reduce(MXT[:, 0:1], IT3, AX.X, add))
            tt(IT2, IT3, CNT, mul)
            d(v.tensor_reduce(MXT[:, 1:2], IT2, AX.X, add))
            tt(IT4, CX, IT1, sub)
            tt(IT4, IT4, IT3, mul)
            d(v.tensor_reduce(MXT[:, 3:4], IT4, AX.X, add))
            ts(MXT[:, 4:5], IOP, float(W), None, mul)
            tt(MXT[:, 3:4], MXT[:, 3:4], MXT[:, 4:5], add)
            tt(ITE[:, 2:3], MXT[:, 3:4], MXT[:, 0:1], mul)
            ts(MXT[:, 2:3], IOP, -float(W), None, mul)
            tt(MXT[:, 1:2], MXT[:, 1:2], MXT[:, 2:3], add)
            ts(MXT[:, 1:2], MXT[:, 1:2], 1.0, float(W), ALU.max, ALU.min)
            tt(ITE[:, 1:2], MXT[:, 1:2], MXT[:, 0:1], mul, s=ite_done)
            wait_filled(dve, ("itm",))
            evac(dve, v.tensor_copy(ITM, bank(("itm",))[0:1, 0:3 * P]), ("itm",), own=True)
            dve.sem_inc(itm_done, 1)
            for l in range(L):
                for c in range(2):
                    u = ("bd", l, c)
                    cc = slice(c * HALF, (c + 1) * HALF)
                    wait_filled(dve, u)
                    evac(dve, v.tensor_tensor(H[:, l, cc], bank(u), H[:, l, cc], add), u, own=True)
            dve.wait_ge(tb_in, 16)
            d(v.tensor_copy(TBF[0:NROW, :], TBI[0:NROW, :]), tbf_done)
            wait_filled(dve, ("idx",))
            evac(dve, v.tensor_copy(IDX[:, 0:NROW], bank(("idx",))[:, 0:NROW]), ("idx",), own=True)
            dve.sem_inc(idx_done, 1)

            dve.sem_inc(gb_free, 2)
            dve.sem_inc(dn_split, 4)
            with items(dve) as i:
                n_i = item_tokens(dve, i)
                e_i = item_expert(dve, i)

                def item(n):
                    v.tensor_copy(BGC, BGU[:, bass.ds(e_i * (2 * FT), 2 * FT)]).then_inc(bgc_done, 1)
                    dve.wait_ge(bgc_done, i + 1)

                    def finish(f):
                        b = f % 2
                        dve.wait_ge(si_done, 8 * i + f + 1)
                        v.tensor_tensor(GA[:, b, 0:n], GA[:, b, 0:n], SI[:, b, 0:n], mul).then_inc(ffn_step, 1)
                        dve.wait_ge(ffn_step, 16 * i + 2 * f + (3 if f < FT - 1 else 2))
                        v.tensor_tensor(GA[:, b, 0:n], GA[:, b, 0:n], UP[:, b, 0:n], mul).then_inc(hid_done, 1)
                        dve.wait_ge(hid_done, 16 * i + 2 * f + 1)
                        v.tensor_copy(HTH[:, f, 0:n], GA[:, b, 0:n]).then_inc(hid_done, 1)
                        dve.wait_ge(hid_done, 16 * i + 2 * f + 2)
                        v.tensor_tensor(HTL[:, f, 0:n], GA[:, b, 0:n], HTH[:, f, 0:n].bitcast(F32), sub) \
                            .then_inc(ht_done, 1)

                    def low(k):
                        dve.wait_ge(dn_high, 8 * i + k + 1)
                        v.tensor_tensor(DNL[:, k % 4, :], DNW[:, k // 2 % 2, k % 2, :],
                                        DNH[:, k % 4, :].bitcast(F32), sub).then_inc(dn_split, 1)

                    for f in range(FT):
                        b = f % 2
                        if f >= 2:
                            dve.wait_ge(ht_done, 8 * i + f - 1)
                        dve.wait_ge(gb_filled, 8 * i + f + 1)
                        v.tensor_scalar(GA[:, b, 0:n], PS[:, b, 0:n], BGC[:, f:f + 1], LIMIT, add, ALU.min) \
                            .then_inc(ga_done, 1)
                        v.tensor_scalar(UP[:, b, 0:n], PS[:, b, W:W + n], BGC[:, FT + f:FT + f + 1], LIMIT,
                                        add, ALU.min).then_inc(gb_free, 1)
                        dve.wait_ge(gb_free, 8 * i + f + 3)
                        v.tensor_scalar(UP[:, b, 0:n], UP[:, b, 0:n], -LIMIT, 1.0, ALU.max, add).then_inc(ffn_step, 1)
                        if f:
                            finish(f - 1)
                        if 1 <= f <= 4:
                            low(f - 1)
                    finish(FT - 1)
                    for k in range(4, FT):
                        low(k)

                by_width(dve, n_i, item)

            dve.wait_ge(fg_in, 16)

            def last_norm(l):
                dve.wait_ge(ssq_done[4], l + 1)
                d(v.reciprocal(sm[:, l + 16:l + 17], sm[:, l + 8:l + 9]), rstd_done[4])
                if l >= POOL_TILES:
                    stt(H[:, l, :], H[:, l, :], sm[:, l + 16:l + 17], FG, mul, mul, s=out_ready_dve)

            for l in range(L):
                dve.wait_ge(cb_in[l % 4], 16 * TOPK * (l // 4 + 1))
                for j in range(TOPK):
                    stt(H[:, l, :], CB[:, l % 4, j, :], GW[:, l, j:j + 1], H[:, l, :], mul, add,
                        s=comb_done if j == TOPK - 1 else dve_step)
                if l:
                    last_norm(l - 1)
            last_norm(L - 1)

        @block.gpsimd
        def _(pool):
            g = nc.gpsimd
            mul, add, sub = ALU.mult, ALU.add, ALU.subtract

            def d(ins, s=pool_step):
                link(pool, ins, s)

            def tt(o, x, y, op, s=pool_step):
                d(g.tensor_tensor(o, x, y, op), s)

            d(g.memset(ident[:], 0.0))
            d(g.affine_select(out=ident[:], in_=ident[:], compare_op=ALU.not_equal, fill=1.0, base=0,
                              pattern=[[-1, P]], channel_multiplier=1), consts)
            d(g.memset(ones[:], 1.0), consts)
            for t in (BA, BX, BG):
                d(g.memset(t, 0.0), zeroed)
            d(g.iota(IOI, pattern=[[1, E]], base=0, channel_multiplier=0))
            d(g.tensor_copy(IO, IOI), iota_done)
            d(g.iota(IOI[:, 0:1], pattern=[[1, 1]], base=0, channel_multiplier=1))
            d(g.tensor_copy(IOP, IOI[:, 0:1]), iota_done)
            d(g.iota(TOKI, pattern=[[1, L]], base=0, channel_multiplier=L), iota_done)
            pool.wait_ge(d_in, 16)
            d(g.affine_select(out=DB.rearrange("p (g c) -> p g c", g=G), in_=DB.rearrange("p (g c) -> p g c", g=G),
                              compare_op=ALU.is_equal, fill=0.0, base=-(L - 1) * SC,
                              pattern=[[0, G], [-1, SC]], channel_multiplier=1), db_done)

            pool.wait_ge(bb_done, 1)

            def b4(x):
                return x.unsqueeze(2).to_broadcast([P, Q, L, SC])

            def p4(x):
                return x.unsqueeze(3).to_broadcast([P, Q, L, SC])

            TG1 = wa(8192, Q, L, SC)
            TG2 = wa(8192 + 2048, Q, L, SC)
            for r in range(2):
                tt(TG1, p4(QV[:, 0]), b4(BB[:, r]), mul)
                tt(TG2, p4(QV[:, 1]), b4(BB[:, 1 - r]), mul)
                tt(GM[:, r], TG1, TG2, add if r else sub, s=g_done if r else pool_step)
            pool.wait_ge(kts_done, 1)
            d(g.memset(RT[:, 0, :, 0:1], 1.0))
            d(g.memset(RT[:, 1, :, 0:1], 0.0))
            uc, us = sm[:, 144:160], sm[:, 160:176]
            n = 1
            while n < P:
                t1, t2 = TG1.rearrange("p a b c -> p (a b c)"), TG2.rearrange("p a b c -> p (a b c)")
                t1 = t1[:, 0:Q * n].rearrange("p (q n) -> p q n", q=Q)
                t2 = t2[:, 0:Q * n].rearrange("p (q n) -> p q n", q=Q)
                c, s_ = (x.unsqueeze(2).to_broadcast([P, Q, n]) for x in (uc, us))
                tt(t1, RT[:, 0, :, 0:n], c, mul)
                tt(t2, RT[:, 1, :, 0:n], s_, mul)
                tt(RT[:, 0, :, n:2 * n], t1, t2, sub)
                tt(t1, RT[:, 0, :, 0:n], s_, mul)
                tt(t2, RT[:, 1, :, 0:n], c, mul)
                tt(RT[:, 1, :, n:2 * n], t1, t2, add)
                n *= 2
                if n < P:
                    a1, a2, a3 = (TG1.rearrange("p a b c -> p (a b c)")[:, Q * k:Q * k + Q] for k in range(3))
                    tt(a1, uc, uc, mul)
                    tt(a2, us, us, mul)
                    tt(a3, uc, us, mul)
                    tt(uc, a1, a2, sub)
                    tt(us, a3, a3, add)
            pool.sem_inc(rot_done, 1)
            d(g.memset(MM, 0.0))
            pool.dma_start(slot_tok.rearrange("(r p) o -> r (p o)", p=P),
                           MM[0:NROW, 0, 0:P].bitcast(I32)).then_inc(zero_out, 16)
            pool.wait_ge(zero_out, 16)
            for l in range(L):
                pool.dma_start(MM[0:(l + 1) * SC, l, :], KTS[(L - 1 - l) * SC:P, :]).then_inc(mm_in, 16)
            pool.wait_ge(rg_done, CT)
            wait_filled(pool, ("ut", 7))
            TF1 = YTf[:, 5120:6144].rearrange("p (q l c) -> p q l c", q=Q // 2, l=L)
            TF2 = YTf[:, 6144:7168].rearrange("p (q l c) -> p q l c", q=Q // 2, l=L)
            for hq in range(2):
                qs = slice(hq * Q // 2, (hq + 1) * Q // 2)
                sh = [P, Q // 2, L, SC]
                c0, c1 = (CC[:, r, qs].unsqueeze(2).to_broadcast(sh) for r in range(2))
                w0, w1 = (PW[:, r, qs, 1:9].unsqueeze(3).to_broadcast(sh) for r in range(2))
                tt(TF1, c0, w0, mul)
                tt(TF2, c1, w1, mul)
                tt(FM[:, 0, qs], TF1, TF2, add)
                tt(TF1, c1, w0, mul)
                tt(TF2, c0, w1, mul)
                tt(FM[:, 1, qs], TF1, TF2, sub, s=f_done)
            pool.wait_ge(h2_done, 2 * L)
            d(g.affine_select(out=TRI, in_=ones[:], compare_op=ALU.is_gt, fill=0.0, base=0,
                              pattern=[[1, P]], channel_multiplier=-1), tri_done)
            pool.wait_ge(pos_done, 1)
            for j in range(TOPK):
                for l in range(L):
                    g.indirect_dma_start(out=slot_tok[:, :],
                                         out_offset=bass.IndirectOffsetOnAxis(ap=POS[:, j * L + l:j * L + l + 1], axis=0),
                                         in_=TOKI[:, l:l + 1], in_offset=None).then_inc(scat, 16)
            pool.wait_ge(scat, 16 * TOPK * L)
            pool.wait_ge(xn_out, 16 * L)

            def gather(tiles):
                for t in range(tiles):
                    g.indirect_dma_start(out=XG[:, t, :], out_offset=None, in_=xn_rows[:, :],
                                         in_offset=bass.IndirectOffsetOnAxis(ap=IDC[:, t:t + 1], axis=0)) \
                        .then_inc(xg_in, 32 // tiles)

            pool.wait_ge(idx_done, 1)
            pool.wait_ge(itm_done, 1)
            g.memset(YS[:, 1, :], 0.0).then_inc(y_zero, 1)
            pool.wait_ge(y_zero, 1)
            pool.sem_inc(ys_free, 1)
            g.tensor_copy(IDC, IDX[:, 0:2]).then_inc(idc_done, 1)
            pool.wait_ge(idc_done, 1)
            gather(2)
            with items(pool) as i:
                n_i = item_tokens(pool, i)
                n_next = item_tokens(pool, i + 1)

                def row(t):
                    return pool.value_load(ITM[0:1, bass.ds(i + 2 * P, 1)], min_val=0, max_val=T * TOPK) + t * P

                def fetch_and_store(store):
                    pool.wait_ge(xg_in, 32 * i + 32)
                    g.tensor_copy(IDC, IDX[:, bass.ds(2 * i + 2, 2)]).then_inc(idc_done, 1)
                    pool.wait_ge(idc_done, i + 2)
                    pool.wait_ge(xe_filled, 4 * i + 4)
                    pool.sem_inc(gather_go, 1)
                    with pool.If(n_next > P):
                        gather(2)
                    with pool.Else():
                        gather(1)
                    pool.wait_ge(y_done, i + 2)
                    store()
                    pool.wait_ge(y_out, 32 * i + 32)
                    pool.sem_inc(ys_free, 1)

                def store_one():
                    pool.dma_start(y_rows[bass.ds(row(0), P), :], YS[:, 0, :]).then_inc(y_out, 32)

                def store_two():
                    pool.dma_start(y_rows[bass.ds(row(0), P), :], YS[:, 0, :]).then_inc(y_out, 16)
                    pool.dma_start(y_rows[bass.ds(row(1), P), :], YS[:, 1, :]).then_inc(y_out, 16)

                with pool.If(n_i > 0):
                    with pool.If(n_i > P):
                        fetch_and_store(store_two)
                    with pool.Else():
                        fetch_and_store(store_one)
            for l in range(L):
                if l >= 4:
                    pool.wait_ge(comb_done, l - 3)
                for j in range(TOPK):
                    g.indirect_dma_start(out=CB[:, l % 4, j, :], out_offset=None, in_=y_rows[0:T * TOPK, :],
                                         in_offset=bass.IndirectOffsetOnAxis(ap=POSY[:, j * L + l:j * L + l + 1], axis=0)) \
                        .then_inc(cb_in[l % 4], 16)
            pool.wait_ge(fg_in, 16)
            for l in range(POOL_TILES):
                pool.wait_ge(last_scaled, l + 1)
                g.tensor_tensor(H[:, l, :], H[:, l, :], FG, mul).then_inc(out_ready, 1)


def kernel(**inputs):
    import numpy as _np
    import concourse.bacc as _bacc
    from concourse import mybir as _mybir
    from concourse.bass_utils import run_bass_kernel_spmd as _run

    nc = _bacc.Bacc("TRN2", target_bir_lowering=False, num_devices=1)
    arrays, args = {}, {}
    for name in NAMES:
        a = _np.ascontiguousarray(inputs[name])
        arrays[f"in_{name}"] = a
        args[name] = nc.dram_tensor(f"in_{name}", a.shape, _mybir.dt.from_np(a.dtype), kind="ExternalInput").ap()
    out = nc.dram_tensor("out", arrays["in_x"].shape, _mybir.dt.float32, kind="ExternalOutput").ap()
    build(nc, args, out)
    return _run(nc, [arrays], core_ids=[0]).results[0]["out"]
```
